# Optimizing a Trainium2 kernel written in Bass

```python
import math
import jax, jax.numpy as jnp
from jax import lax
import numpy as np

D_MODEL = 1024
BATCH = 1
SEQ = 2048
DEPTH = 1

POOL_WINDOWS = (2, 4, 8, 16)
POOL_GROUP = D_MODEL // 16
D_A = POOL_GROUP * len(POOL_WINDOWS)
N_HEADS = 8
HEAD_DIM = 64
D_B = N_HEADS * HEAD_DIM
Q_BLOCK = 128
SSM_GROUP = 16
D_C = D_MODEL // 4
SSM_GROUPS = D_C // SSM_GROUP
SSM_STATE = 64
DT_MIN = 0.001
DT_MAX = 0.1
DEEPNORM_ALPHA = (2.0 * DEPTH) ** 0.25
DEEPNORM_BETA = (8.0 * DEPTH) ** -0.25
LN_EPS = 1e-5
N_BRANCHES = 3

IN_SIZES = (D_A, D_A,
            D_B, D_B, D_B,
            N_HEADS,
            D_B,
            D_C, D_C,
            N_BRANCHES * D_MODEL)
IN_SPLITS = tuple(int(v) for v in np.cumsum(IN_SIZES)[:-1])
D_IN = int(sum(IN_SIZES))
F_OFFSET = D_A * 2 + D_B * 3

kernel_name = "hybrid_pool_fox_s5_gated_deepnorm"

def layer_norm(x, g, b):
    xf = x.astype(jnp.float32)
    mu = jnp.mean(xf, axis=-1, keepdims=True)
    var = jnp.mean(jnp.square(xf - mu), axis=-1, keepdims=True)
    y = (xf - mu) * lax.rsqrt(var + LN_EPS) * g.astype(jnp.float32) + b.astype(jnp.float32)
    return y.astype(x.dtype)

def pool_mixer(u, pool_w, pool_scale):
    b, s, _ = u.shape
    uf = u.astype(jnp.float32).reshape(b, s, len(POOL_WINDOWS), POOL_GROUP)
    csum = jnp.cumsum(uf, axis=1)
    pos = jnp.arange(s)
    outs = []
    for gi, w in enumerate(POOL_WINDOWS):
        cg = csum[:, :, gi]
        shifted = jnp.concatenate([jnp.zeros((b, w, POOL_GROUP), jnp.float32), cg], axis=1)[:, :s]
        count = jnp.minimum(pos + 1, w).astype(jnp.float32)[None, :, None]
        pooled = (cg - shifted) / count - uf[:, :, gi]
        outs.append(jnp.einsum('bsc,ce->bse', pooled, pool_w[gi].astype(jnp.float32)))
    y = jnp.concatenate(outs, axis=-1) * pool_scale.astype(jnp.float32)
    return y

def fox_attention(q, k, v, f_logit):
    b, s, h, dh = q.shape
    nb = s // Q_BLOCK
    logf = jax.nn.log_sigmoid(f_logit.astype(jnp.float32))
    fcum = jnp.cumsum(logf, axis=1)
    fk = jnp.transpose(fcum, (0, 2, 1))
    qb = jnp.moveaxis(q.reshape(b, nb, Q_BLOCK, h, dh), 1, 0)
    fqb = jnp.moveaxis(fcum.reshape(b, nb, Q_BLOCK, h), 1, 0)
    key_pos = jnp.arange(s)
    scale = 1.0 / math.sqrt(dh)

    def one_block(args):
        qi, fqi, bi = args
        scores = jnp.einsum('bqhd,bkhd->bhqk', qi, k,
                            preferred_element_type=jnp.float32) * scale
        bias = jnp.transpose(fqi, (0, 2, 1))[..., None] - fk[:, :, None, :]
        q_pos = bi * Q_BLOCK + jnp.arange(Q_BLOCK)
        mask = key_pos[None, :] <= q_pos[:, None]
        logits = jnp.where(mask[None, None], scores + bias, -jnp.inf)
        p = jax.nn.softmax(logits, axis=-1)
        return jnp.einsum('bhqk,bkhd->bqhd', p, v.astype(jnp.float32))

    out = lax.map(one_block, (qb, fqb, jnp.arange(nb)))
    return jnp.moveaxis(out, 0, 1).reshape(b, s, h * dh)

def _ssm_combine(e1, e2):
    a1r, a1i, b1r, b1i = e1
    a2r, a2i, b2r, b2i = e2
    ar = a1r * a2r - a1i * a2i
    ai = a1r * a2i + a1i * a2r
    br = a2r * b1r - a2i * b1i + b2r
    bi = a2r * b1i + a2i * b1r + b2i
    return (ar, ai, br, bi)

def s5_mixer(u, a_re, a_im, log_dt, b_re, b_im, c_re, c_im, d_skip, w_glu, b_glu):
    b, s, _ = u.shape
    uf = u.astype(jnp.float32)
    ug = uf.reshape(b, s, SSM_GROUPS, SSM_GROUP)
    are = a_re.astype(jnp.float32)
    aim = a_im.astype(jnp.float32)
    dt = jnp.exp(log_dt.astype(jnp.float32))[:, None]
    mag = jnp.exp(are * dt)
    ang = aim * dt
    abar_re = mag * jnp.cos(ang)
    abar_im = mag * jnp.sin(ang)
    den = are * are + aim * aim
    nr = abar_re - 1.0
    coef_re = (nr * are + abar_im * aim) / den
    coef_im = (abar_im * are - nr * aim) / den
    br_ = b_re.astype(jnp.float32)
    bi_ = b_im.astype(jnp.float32)
    bb_re = coef_re[..., None] * br_ - coef_im[..., None] * bi_
    bb_im = coef_re[..., None] * bi_ + coef_im[..., None] * br_
    bu_re = jnp.einsum('bsgh,gph->bsgp', ug, bb_re)
    bu_im = jnp.einsum('bsgh,gph->bsgp', ug, bb_im)
    a_full_re = jnp.broadcast_to(abar_re, bu_re.shape)
    a_full_im = jnp.broadcast_to(abar_im, bu_im.shape)
    _, _, xr, xi = lax.associative_scan(_ssm_combine, (a_full_re, a_full_im, bu_re, bu_im), axis=1)
    y = (jnp.einsum('ghp,bsgp->bsgh', c_re.astype(jnp.float32), xr)
         - jnp.einsum('ghp,bsgp->bsgh', c_im.astype(jnp.float32), xi)).reshape(b, s, D_C)
    y = y + d_skip.astype(jnp.float32) * uf
    y = jax.nn.gelu(y)
    return y * jax.nn.sigmoid(jnp.einsum('bsc,ce->bse', y, w_glu.astype(jnp.float32))
                              + b_glu.astype(jnp.float32))

def hybrid_layer(x, w_in, b_in, pool_w, pool_scale, a_re, a_im, log_dt, b_re, b_im, c_re, c_im,
                 d_skip, w_glu, b_glu, w_up_a, w_up_b, w_up_c, w_out, ln_g, ln_b):
    b, s, _ = x.shape
    z = jnp.einsum('bsd,de->bse', x, w_in) + b_in
    (za, ga, zq, zk, zv, zf, gb, zc, gc, zg) = jnp.split(z, IN_SPLITS, axis=-1)
    gaf = ga.astype(jnp.float32)
    gbf = gb.astype(jnp.float32)
    gcf = gc.astype(jnp.float32)
    y_a = pool_mixer(za, pool_w, pool_scale) * jax.nn.silu(gaf)
    y_b = fox_attention(zq.reshape(b, s, N_HEADS, HEAD_DIM), zk.reshape(b, s, N_HEADS, HEAD_DIM),
                        zv.reshape(b, s, N_HEADS, HEAD_DIM), zf) * jax.nn.silu(gbf)
    y_c = s5_mixer(zc, a_re, a_im, log_dt, b_re, b_im, c_re, c_im, d_skip, w_glu, b_glu) \
        * jax.nn.silu(gcf)
    gates = jax.nn.sigmoid(zg.astype(jnp.float32)).reshape(b, s, N_BRANCHES, D_MODEL)
    merged = (gates[:, :, 0] * jnp.einsum('bsc,cd->bsd', y_a, w_up_a.astype(jnp.float32))
              + gates[:, :, 1] * jnp.einsum('bsc,cd->bsd', y_b, w_up_b.astype(jnp.float32))
              + gates[:, :, 2] * jnp.einsum('bsc,cd->bsd', y_c, w_up_c.astype(jnp.float32)))
    out = jnp.einsum('bsd,de->bse', merged, w_out.astype(jnp.float32))
    return layer_norm((DEEPNORM_ALPHA * x.astype(jnp.float32) + out).astype(x.dtype), ln_g, ln_b)

def setup_inputs(seed: int = 0) -> dict:
    key = jax.random.key(seed)
    ks = jax.random.split(key, 24)
    L = DEPTH
    f32 = jnp.float32
    x = jax.random.normal(ks[0], (BATCH, SEQ, D_MODEL), f32)
    w_in = jax.random.normal(ks[1], (L, D_MODEL, D_IN), f32) * D_MODEL ** -0.5
    b_in = 0.02 * jax.random.normal(ks[2], (L, D_IN), f32)
    f_bias = jnp.linspace(1.0, 5.0, N_HEADS)[None, :] + 0.1 * jax.random.normal(ks[3], (L, N_HEADS), f32)
    b_in = b_in.at[:, F_OFFSET:F_OFFSET + N_HEADS].set(f_bias)
    pool_w = jax.random.normal(ks[4], (L, len(POOL_WINDOWS), POOL_GROUP, POOL_GROUP), f32) * POOL_GROUP ** -0.5
    pool_scale = 1.0 + 0.1 * jax.random.normal(ks[5], (L, D_A), f32)
    n_idx = jnp.arange(SSM_STATE, dtype=f32)[None, None, :]
    ssm_a_re = -0.5 + 0.01 * jax.random.normal(ks[6], (L, SSM_GROUPS, SSM_STATE), f32)
    ssm_a_im = math.pi * n_idx + 0.01 * jax.random.normal(ks[7], (L, SSM_GROUPS, SSM_STATE), f32)
    ssm_log_dt = jax.random.uniform(ks[8], (L, SSM_GROUPS), f32, math.log(DT_MIN), math.log(DT_MAX))
    bs = (2.0 * SSM_GROUP) ** -0.5
    ssm_b_re = jax.random.normal(ks[9], (L, SSM_GROUPS, SSM_STATE, SSM_GROUP), f32) * bs
    ssm_b_im = jax.random.normal(ks[10], (L, SSM_GROUPS, SSM_STATE, SSM_GROUP), f32) * bs
    cs = (2.0 * SSM_STATE) ** -0.5
    ssm_c_re = jax.random.normal(ks[11], (L, SSM_GROUPS, SSM_GROUP, SSM_STATE), f32) * cs
    ssm_c_im = jax.random.normal(ks[12], (L, SSM_GROUPS, SSM_GROUP, SSM_STATE), f32) * cs
    ssm_d = jax.random.normal(ks[13], (L, D_C), f32)
    w_glu = jax.random.normal(ks[14], (L, D_C, D_C), f32) * D_C ** -0.5
    b_glu = 0.02 * jax.random.normal(ks[15], (L, D_C), f32)
    w_up_a = jax.random.normal(ks[16], (L, D_A, D_MODEL), f32) * (D_A ** -0.5) * DEEPNORM_BETA
    w_up_b = jax.random.normal(ks[17], (L, D_B, D_MODEL), f32) * (D_B ** -0.5) * DEEPNORM_BETA
    w_up_c = jax.random.normal(ks[18], (L, D_C, D_MODEL), f32) * (D_C ** -0.5) * DEEPNORM_BETA
    w_out = jax.random.normal(ks[19], (L, D_MODEL, D_MODEL), f32) * (D_MODEL ** -0.5) * DEEPNORM_BETA
    ln_g = 1.0 + 0.05 * jax.random.normal(ks[20], (L, D_MODEL), f32)
    ln_b = 0.02 * jax.random.normal(ks[21], (L, D_MODEL), f32)
    return {"x": x, "w_in": w_in, "b_in": b_in, "pool_w": pool_w, "pool_scale": pool_scale,
            "ssm_a_re": ssm_a_re, "ssm_a_im": ssm_a_im, "ssm_log_dt": ssm_log_dt,
            "ssm_b_re": ssm_b_re, "ssm_b_im": ssm_b_im, "ssm_c_re": ssm_c_re, "ssm_c_im": ssm_c_im,
            "ssm_d": ssm_d, "w_glu": w_glu, "b_glu": b_glu, "w_up_a": w_up_a, "w_up_b": w_up_b,
            "w_up_c": w_up_c, "w_out": w_out, "ln_g": ln_g, "ln_b": ln_b}

def reference(x, w_in, b_in, pool_w, pool_scale, ssm_a_re, ssm_a_im, ssm_log_dt, ssm_b_re, ssm_b_im,
              ssm_c_re, ssm_c_im, ssm_d, w_glu, b_glu, w_up_a, w_up_b, w_up_c, w_out, ln_g, ln_b):
    h = x
    for l in range(DEPTH):
        h = hybrid_layer(h, w_in[l], b_in[l], pool_w[l], pool_scale[l], ssm_a_re[l], ssm_a_im[l],
                         ssm_log_dt[l], ssm_b_re[l], ssm_b_im[l], ssm_c_re[l], ssm_c_im[l], ssm_d[l],
                         w_glu[l], b_glu[l], w_up_a[l], w_up_b[l], w_up_c[l], w_out[l], ln_g[l], ln_b[l])
    return h


_drawn_inputs = setup_inputs


def setup_inputs(seed=0):
    import zlib

    import numpy as np

    out = dict(_drawn_inputs(seed))
    spreads = {}
    factors = {'pool_scale': 6.354,
     'ssm_a_re': 64.0,
     'ssm_a_im': 64.0,
     'ssm_log_dt': 64.0,
     'ssm_b_re': 64.0,
     'ssm_b_im': 64.0,
     'ssm_c_re': 64.0,
     'ssm_c_im': 64.0,
     'w_glu': 5.471,
     'b_glu': 64.0,
     'ln_b': 2.756}
    for name, (base, spread) in spreads.items():
        noise = np.random.default_rng([zlib.crc32(name.encode()), seed]).standard_normal(out[name].shape)
        drawn = base * np.exp(spread * noise) if base else spread * noise
        out[name] = __import__('jax').numpy.asarray(drawn.astype(out[name].dtype))
    for name, factor in factors.items():
        out[name] = (out[name] * factor).astype(out[name].dtype)
    return out
```

```python
from contextlib import ExitStack

import numpy as np

import concourse.bass as bass
from concourse import mybir

F32 = mybir.dt.float32
F32R = mybir.dt.float32r
BF16 = mybir.dt.bfloat16
ACT = mybir.ActivationFunctionType
ALU = mybir.AluOpType
AX_X = mybir.AxisListType.X

P = 128
D = 1024
S = 2048
KT = D // P
HALF = S // 2
BANK = 512
NCH = HALF // BANK
WINDOWS = (2, 4, 8, 16)
POOL_C = 64
HEADS = 8
HD = 64
D_B = HEADS * HD
D_C = D // 4
GROUPS, GC, STATES = 16, 16, 64
TAU = 8
CHUNKS = HALF // TAU
ALPHA = 2.0 ** 0.25
EPS = 1e-5

T_ZA, T_SIL, T_QKV, T_GATE = 2, 8, 12, 24
T_HALF = T_ZA + T_SIL + T_QKV
ZCF = D_C + HEADS
TWO_PI = 6.283185307179586
PI_A = 6.28125
PI_B = 0.0019350051879882812
PI_C = TWO_PI - PI_A - PI_B
ROUND = 1.5 * 2.0 ** 23


def low_with_raw(nc, ctx, name, shape):
    low = ctx.enter_context(nc.sbuf_tensor(name, shape, F32R))
    raw = nc.alloc_sbuf_tensor_at(name + "_raw", shape, F32, offset=nc.sbuf_base - 4 * int(np.prod(shape[1:])))
    return low, raw


def stage_project(nc, io, scr, ident, x_hi, x_lo, x_raw):
    with ExitStack() as ctx:
        def sb(name, shape, dt=F32):
            return ctx.enter_context(nc.sbuf_tensor(name, shape, dt))

        def sem(name):
            return ctx.enter_context(nc.semaphore(name))

        w_hi = [sb(f"w_hi{i}", [P, KT, P], F32R) for i in range(2)]
        w_lo, w_raw = zip(*(low_with_raw(nc, ctx, f"w_lo{i}", [P, KT, P]) for i in range(2)))
        wcf_hi = sb("wcf_hi", [P, KT, ZCF], F32R)
        wcf_lo, wcf_raw = low_with_raw(nc, ctx, "wcf_lo", [P, KT, ZCF])
        bias = sb("bias", [P, T_HALF])
        bcf = sb("bcf", [P, ZCF])
        sig = sb("sig", [P, HALF])
        zout = [sb(f"zout{i}", [P, HALF]) for i in range(2)]
        pool_u = [sb(f"pool_u{i}", [P, 16 + HALF]) for i in range(2)]
        carry = sb("carry", [P, 2, 16])
        pool_w = sb("pool_w", [P, 2, P])
        pool_s = sb("pool_s", [P, 2])
        pool_edge = sb("pool_edge", [P, 2, 16])
        tmp = sb("tmp", [P, 2, 16 + HALF])
        pool_a, pool_b = tmp[:, 0, :], tmp[:, 1, :]
        zs = sb("zs", [P, GROUPS, TAU, GC])
        zs_flat = zs[:].rearrange("p g t h -> p (g t h)")
        zs_y = zs_flat.rearrange("p (t c) -> p t c", t=TAU)
        glu_v = zs_flat.rearrange("p (e t) -> p e t", e=2)
        u_sb = sb("u_sb", [P, GROUPS, CHUNKS])
        yT = u_sb[:].rearrange("p g c -> p (g c)").rearrange("p (j t) -> p j t", j=2)
        xs = sb("xs", [P, GROUPS, CHUNKS + 1])
        xw = sb("xw", [P, GROUPS, CHUNKS + 1])
        m_in = sb("m_in", [P, GROUPS, P])
        m_out = sb("m_out", [P, GROUPS, TAU + 1, GC])
        toep = sb("toep", [P, GROUPS, P])
        kern = xw[0:GC, :, 0:P]
        fcum = m_in[0:HEADS].rearrange("p g c -> p (g c)")
        bx, by, cx, cy, bb, bw = (sb(n, [P, GROUPS, GC]) for n in ("bx", "by", "cx", "cy", "bb", "bw"))
        dT = sb("dT", [GC, GROUPS])
        (are, aim, dt, mag, ang, rnd, red, sn, sh, den, abr, abi, nr, t0, t1, t2, t3, cr, ci) = (
            sb(n, [P, GROUPS]) for n in ("are", "aim", "dt", "mag", "ang", "rnd", "red", "sn", "sh", "den", "abr",
                                         "abi", "nr", "t0", "t1", "t2", "t3", "cr", "ci"))
        pw_r, pw_i, po_r, po_i = (sb(n, [P, GROUPS, TAU + 1]) for n in ("pw_r", "pw_i", "po_r", "po_i"))
        rv_r, rv_i = (sb(n, [P, GROUPS, TAU]) for n in ("rv_r", "rv_i"))
        q_r, q_i, q_s = (sb(n, [P, 7, GROUPS]) for n in ("q_r", "q_i", "q_s"))
        sgn = sb("sgn", [P, 2])
        glu_w = sb("glu_w", [P, 2, D_C])
        glu_b = sb("glu_b", [P, 2])
        zf = sb("zf", [P, 2, TAU, HEADS])
        zf_m = sb("zf_m", [P, 2, TAU, HEADS])
        one = sb("one", [HEADS, 1])

        tile_ps = [ctx.enter_context(nc.psum_tensor(f"tile_ps{i}", [P, HALF], F32)) for i in range(2)]
        aux_ps = [ctx.enter_context(nc.psum_tensor(f"aux_ps{i}", [P, BANK], F32)) for i in range(4)]

        x_loaded = [sem(f"x_loaded{k}") for k in range(KT)]
        w_loaded = [sem(f"w_loaded{i}") for i in range(2)]
        z_stored = [sem(f"z_stored{i}") for i in range(2)]
        (x_split_hi, x_split, w_split_hi, w_split, cf_loaded, cf_split_hi, cf_split, consts, pool_w_zero, pool_w_in,
         tile_done, tile_out, sig_ready, aux_full, aux_free, pool_stored, glu_stored, dve_step, pool_step, act_step, dt_ready,
         arg_ready, mag_ready, ang_ready, sin_ready, coefs, in_table, out_table, kern_ready, toep_zero, toep_set,
         pooled, v_ready, scanned, glu_in, glu_sig, glu_out, yT_in, gelu_done, pool_out, f_arg, f_exp, f_ln,
         f_done, f_stored) = (
            sem(n) for n in (
                "x_split_hi", "x_split", "w_split_hi", "w_split", "cf_loaded", "cf_split_hi", "cf_split", "consts",
                "pool_w_zero", "pool_w_in", "tile_done", "tile_out", "sig_ready", "aux_full", "aux_free",
                "pool_stored", "glu_stored", "dve_step", "pool_step", "act_step", "dt_ready", "arg_ready", "mag_ready", "ang_ready",
                "sin_ready", "coefs", "in_table", "out_table", "kern_ready", "toep_zero", "toep_set", "pooled",
                "v_ready", "scanned", "glu_in", "glu_sig", "glu_out", "yT_in", "gelu_done", "pool_out", "f_arg",
                "f_exp", "f_ln", "f_done", "f_stored"))

        uses, at = {}, 0
        for hf in range(2):
            for name, n in (("cf", TAU), ("in_table", 4 * (1 - hf)), ("kern", 4 * (1 - hf)), ("pool", 4), ("u", 4),
                            ("v", 4), ("forget", 4 * hf), ("y", 4), ("yT", 4), ("glu", 4)):
                uses[name, hf] = at
                at += n

        SMALL = [(bias[:], io["b_tiles"][:, 0:T_HALF]), (bcf[:], io["b_cf"].partition_broadcast(P)),
                 (are[0:64], io["a_re"]), (are[64:P], io["a_re"]), (aim[0:64], io["a_im"]), (aim[64:P], io["a_im"]),
                 (dt[:], io["log_dt"].partition_broadcast(P)),
                 (bx[0:64], io["b_re"]), (bx[64:P], io["b_im"]), (by[0:64], io["b_im"]), (by[64:P], io["b_re"]),
                 (cx[0:64], io["c_re"]), (cx[64:P], io["c_im"]), (cy[0:64], io["c_im"]), (cy[64:P], io["c_re"]),
                 (dT[:], io["d_skip"]), (pool_s[:], io["pool_scale"]), (pool_edge[:], io["pool_edge"]),
                 (glu_w[:], io["w_glu"]), (glu_b[:], io["b_glu"])]
        n_consts = 16 * len(SMALL)

        block = ctx.enter_context(nc.Block())

        @block.sync
        def _(sp):
            def load_w(row, n):
                sp.dma_start(w_raw[n % 2][:], row).then_inc(w_loaded[n % 2], 16)

            def store(dst, hf, u, n):
                sp.wait_ge(tile_out, n + 1)
                sp.dma_start(dst[:, hf * HALF:(hf + 1) * HALF], zout[u][:]).then_inc(z_stored[u], 16)

            w_rows = io["w_tiles"].rearrange("m p (k c) -> (m p) k c", c=P)

            def row(i):
                return w_rows[i * P:(i + 1) * P]

            for hf in range(2):
                n0 = hf * T_HALF
                if hf == 0:
                    load_w(row(0), 0)
                else:
                    sp.wait_ge(tile_done, n0)
                for k in range(KT):
                    sp.dma_start(x_raw[:, k, :],
                                 io["xT"][k * P:(k + 1) * P, hf * HALF:(hf + 1) * HALF]).then_inc(x_loaded[k], 16)
                if hf == 0:
                    load_w(row(1), 1)
                    sp.dma_start(wcf_raw[:], io["w_cf"]).then_inc(cf_loaded, 16)
                for i in range(T_ZA):
                    sp.wait_ge(tile_done, n0 + i + 1)
                    load_w(row(i + 2), n0 + i + 2)
                with sp.Fori(0, T_SIL // 2) as i:
                    for u in range(2):
                        sp.wait_ge(tile_done, i * 2 + (n0 + T_ZA + u + 1))
                        load_w(w_rows[bass.ds(i * (2 * P) + (T_ZA + u + 2) * P, P)], u)
                        store(scr["silT"][bass.ds(i * (2 * P) + u * P, P)], hf, u, i * 2 + (n0 + T_ZA + u))
                with sp.Fori(0, T_QKV // 2 - 1) as i:
                    for u in range(2):
                        sp.wait_ge(tile_done, i * 2 + (n0 + T_ZA + T_SIL + u + 1))
                        load_w(w_rows[bass.ds(i * (2 * P) + (T_ZA + T_SIL + u + 2) * P, P)], u)
                        store(scr["qkvT"][bass.ds(i * (2 * P) + u * P, P)], hf, u, i * 2 + (n0 + T_ZA + T_SIL + u))
                for u in range(2):
                    n = n0 + T_HALF - 2 + u
                    if hf == 0:
                        sp.wait_ge(tile_done, n + 1)
                        load_w(row(u), n + 2)
                    store(scr["qkvT"][(T_QKV - 2 + u) * P:(T_QKV - 1 + u) * P], hf, u, n)
            for u in range(2):
                sp.wait_ge(z_stored[u], 16 * (T_SIL + T_QKV))

        @block.scalar
        def _(act):
            def split_w(par, loaded):
                act.wait_ge(w_loaded[par], loaded)
                act.activation(w_hi[par][:], w_raw[par][:], ACT.Copy).then_inc(w_split_hi, 1)

            def split_x(hf, ks):
                for k in ks:
                    act.wait_ge(x_loaded[k], 16 * (hf + 1))
                    act.activation(x_hi[:, k, :], x_raw[:, k, :], ACT.Copy).then_inc(x_split_hi, 1)

            for dst, src in SMALL:
                act.dma_start(dst, src).then_inc(consts, 16)
            for hf in range(2):
                n0 = hf * T_HALF
                if hf == 0:
                    split_w(0, 16)
                    split_x(0, range(KT))
                    split_w(1, 16)
                    act.wait_ge(cf_loaded, 16)
                    act.activation(wcf_hi[:], wcf_raw[:], ACT.Copy).then_inc(cf_split_hi, 1)
                for i in range(T_ZA):
                    split_w(i, 8 * n0 + 32)
                if hf == 0:
                    act.wait_ge(consts, n_consts)
                    act.activation(dt[:], dt[:], ACT.Exp).then_inc(dt_ready, 1)
                    act.wait_ge(arg_ready, 1)
                    act.activation(mag[:], mag[:], ACT.Exp).then_inc(mag_ready, 1)
                    act.wait_ge(ang_ready, 1)
                    act.activation(sn[:], red[:], ACT.Sin).then_inc(sin_ready, 1)
                    act.activation(sh[:], red[:], ACT.Sin, scale=0.5).then_inc(sin_ready, 1)
                with act.Fori(0, T_SIL // 2) as i:
                    for u in range(2):
                        act.wait_ge(tile_done, i * 2 + (n0 + T_ZA + u + 1))
                        act.wait_ge(tile_out, i * 2 + (n0 + T_ZA + u))
                        act.activation(sig[:], tile_ps[u][:], ACT.Sigmoid,
                                       bias=bias[:, bass.ds(i * 2 + (T_ZA + u), 1)]).then_inc(sig_ready, 1)
                        split_w(u, i * 16 + (8 * n0 + 48))
                with act.Fori(0, T_QKV // 2 - 1) as i:
                    for u in range(2):
                        split_w(u, i * 16 + (8 * (n0 + T_SIL) + 48))
                if hf == 0:
                    for u in range(2):
                        split_w(u, 8 * T_HALF + 16)
                    split_x(1, range(KT // 2))
                if hf == 1:
                    act.wait_ge(f_arg, 1)
                    act.activation(zf[:], zf[:], ACT.Exp, scale=-1.0).then_inc(f_exp, 1)
                    act.wait_ge(f_exp, 1)
                    act.activation(zf[:], zf[:], ACT.Ln, bias=1.0).then_inc(f_ln, 1)
                for j in range(2):
                    act.wait_ge(yT_in, 2 * (2 * hf + j + 1))
                    act.activation(yT[:, j, :], yT[:, j, :], ACT.Gelu_apprx_tanh).then_inc(gelu_done, 1)
                for e in range(2):
                    act.wait_ge(glu_in, 2 * (2 * hf + e + 1))
                    act.activation(glu_v[:, e, :], glu_v[:, e, :], ACT.Sigmoid).then_inc(glu_sig, 1)
                if hf == 0:
                    split_x(1, range(KT // 2, KT))

        @block.vector
        def _(dve):
            step = [0]

            def link(ins):
                step[0] += 1
                ins.then_inc(dve_step, 1)
                dve.wait_ge(dve_step, step[0])

            def split_w(par, n):
                dve.wait_ge(w_split_hi, n + 1)
                dve.tensor_tensor(w_lo[par][:], w_raw[par][:], w_hi[par][:].bitcast(F32),
                                  ALU.subtract).then_inc(w_split, 1)

            def split_x(hf, ks):
                for k in ks:
                    dve.wait_ge(x_split_hi, hf * KT + k + 1)
                    dve.tensor_tensor(x_lo[:, k, :], x_raw[:, k, :], x_hi[:, k, :].bitcast(F32),
                                      ALU.subtract).then_inc(x_split, 1)

            def bank(name, hf, i):
                n = uses[name, hf] + i
                dve.wait_ge(aux_full, n + 1)
                return aux_ps[n % 4]

            def discretise():
                tt, ts, stt = dve.tensor_tensor, dve.tensor_scalar, dve.scalar_tensor_tensor
                dve.wait_ge(dt_ready, 1)
                tt(mag[:], are[:], dt[:], ALU.mult).then_inc(arg_ready, 1)
                link(tt(ang[:], aim[:], dt[:], ALU.mult))
                link(ts(rnd[:], ang[:], 1.0 / TWO_PI, ROUND, ALU.mult, ALU.add))
                link(ts(rnd[:], rnd[:], -ROUND, None, ALU.add))
                link(stt(red[:], rnd[:], -PI_A, ang[:], ALU.mult, ALU.add))
                link(stt(red[:], rnd[:], -PI_B, red[:], ALU.mult, ALU.add))
                link(stt(red[:], rnd[:], -PI_C, red[:], ALU.mult, ALU.add))
                ts(red[:], red[:], 3.1415925, -3.1415925, ALU.min, ALU.max).then_inc(ang_ready, 1)
                tt(den[:], are[:], are[:], ALU.mult)
                link(tt(t0[:], aim[:], aim[:], ALU.mult))
                link(tt(den[:], den[:], t0[:], ALU.add))
                link(dve.reciprocal(den[:], den[:]))
                dve.wait_ge(mag_ready, 1)
                dve.wait_ge(sin_ready, 2)
                tt(abi[:], mag[:], sn[:], ALU.mult)
                link(stt(t0[:], sh[:], -2.0, sh[:], ALU.mult, ALU.mult))
                link(tt(t0[:], t0[:], mag[:], ALU.mult))
                link(tt(abr[:], t0[:], mag[:], ALU.add))
                link(ts(nr[:], abr[:], -1.0, None, ALU.add))
                tt(t0[:], nr[:], are[:], ALU.mult)
                tt(t1[:], abi[:], aim[:], ALU.mult)
                tt(t2[:], abi[:], are[:], ALU.mult)
                link(tt(t3[:], nr[:], aim[:], ALU.mult))
                tt(t0[:], t0[:], t1[:], ALU.add)
                link(tt(t2[:], t2[:], t3[:], ALU.subtract))
                tt(cr[:], t0[:], den[:], ALU.mult)
                tt(ci[:], t2[:], den[:], ALU.mult).then_inc(coefs, 1)

            def window_sums(hf):
                N = 16 + HALF
                for i in range(2):
                    u = pool_u[i]
                    dve.tensor_copy(carry[:, i, :], u[:, HALF:N])
                    link(dve.tensor_tensor(pool_a[:, 1:N], u[:, 1:N], u[:, 0:N - 1], ALU.add))
                    link(dve.tensor_tensor(pool_b[:, 3:N], pool_a[:, 3:N], pool_a[:, 1:N - 2], ALU.add))
                    if i == 1:
                        link(dve.tensor_tensor(pool_a[:, 7:N], pool_b[:, 7:N], pool_b[:, 3:N - 4], ALU.add))
                        link(dve.tensor_tensor(pool_b[64:P, 15:N], pool_a[64:P, 15:N], pool_a[64:P, 7:N - 8], ALU.add))
                    if hf == 0:
                        dve.tensor_tensor(pool_a[0:64, 16:32], pool_a[0:64, 16:32], pool_edge[0:64, i, :], ALU.mult)
                        link(dve.tensor_tensor(pool_b[64:P, 16:32], pool_b[64:P, 16:32], pool_edge[64:P, i, :],
                                               ALU.mult))
                    dve.scalar_tensor_tensor(u[0:64, 16:N], pool_a[0:64, 16:N], 1.0 / WINDOWS[2 * i],
                                             u[0:64, 16:N], ALU.mult, ALU.subtract)
                    link(dve.scalar_tensor_tensor(u[64:P, 16:N], pool_b[64:P, 16:N], 1.0 / WINDOWS[2 * i + 1],
                                                  u[64:P, 16:N], ALU.mult, ALU.subtract))
                dve.nop().then_inc(pooled, 1)

            dve.memset(one[:], 1.0)
            for hf in range(2):
                n0 = hf * T_HALF
                if hf == 0:
                    split_w(0, 0)
                    split_x(0, range(KT))
                    split_w(1, 1)
                    dve.wait_ge(cf_split_hi, 1)
                    dve.tensor_tensor(wcf_lo[:], wcf_raw[:], wcf_hi[:].bitcast(F32),
                                      ALU.subtract).then_inc(cf_split, 1)
                    dve.wait_ge(consts, n_consts)
                for i in range(T_ZA):
                    if hf == 0:
                        dve.memset(pool_u[i][:, 0:16], 0.0)
                    else:
                        dve.wait_ge(pool_stored, 32)
                        dve.tensor_copy(pool_u[i][:, 0:16], carry[:, i, :])
                    dve.wait_ge(tile_done, n0 + i + 1)
                    dve.tensor_scalar(pool_u[i][:, 16:16 + HALF], tile_ps[i][:], bias[:, i:i + 1], None,
                                      ALU.add).then_inc(tile_out, 1)
                    split_w(i, n0 + i + 2)
                for t in range(TAU):
                    ps = bank("cf", hf, t)
                    if hf == 1 and t == 0:
                        dve.wait_ge(glu_stored, 32)
                    dve.tensor_tensor(zs[:, :, t, :], ps[:, 0:D_C].rearrange("p (g h) -> p g h", g=GROUPS),
                                      bcf[:, 0:D_C].rearrange("p (g h) -> p g h", g=GROUPS), ALU.add)
                    dve.tensor_tensor(zf[:, hf, t, :], ps[:, D_C:ZCF], bcf[:, D_C:ZCF],
                                      ALU.add).then_inc(aux_free, 1)
                if hf == 0:
                    discretise()
                window_sums(hf)
                def gated(i, u, first=False):
                    if not first:
                        dve.wait_ge(z_stored[u], i * 16 + 8 * hf * (T_SIL + T_QKV))
                    dve.wait_ge(sig_ready, i * 2 + (hf * T_SIL + u + 1))
                    dve.scalar_tensor_tensor(zout[u][:], tile_ps[u][:], bias[:, bass.ds(i * 2 + (T_ZA + u), 1)],
                                             sig[:], ALU.add, ALU.mult).then_inc(tile_out, 1)
                    split_w(u, i * 2 + (n0 + T_ZA + u + 2))

                if hf == 0:
                    for u in range(2):
                        gated(0, u, first=True)
                with dve.Fori(1 - hf, T_SIL // 2) as i:
                    for u in range(2):
                        gated(i, u)
                if hf == 0:
                    for i in range(4):
                        ps = bank("in_table", 0, i)
                        dve.tensor_copy(m_in[:, 4 * i:4 * i + 4, :].rearrange("p g c -> p (g c)"),
                                        ps[:]).then_inc(aux_free, 1)
                    for i in range(4):
                        ps = bank("kern", 0, i)
                        dve.tensor_copy(kern[:, 4 * i:4 * i + 4, :], ps[0:GC, :].rearrange("p (g c) -> p g c", g=4)
                                        ).then_inc(aux_free, 1)
                    link(dve.tensor_tensor(bb[0:GC, :, :], ident[0:GC, 0:GC].unsqueeze(1).broadcast_to([GC, GROUPS, GC]),
                                           dT[:].unsqueeze(2).broadcast_to([GC, GROUPS, GC]), ALU.mult))
                    dve.wait_ge(aux_free, uses["pool", 0])
                    dve.tensor_tensor(kern[:, :, 0:GC], kern[:, :, 0:GC], bb[0:GC, :, :], ALU.add
                                      ).then_inc(kern_ready, 1)
                for i in range(4):
                    ps = bank("pool", hf, i)
                    dve.tensor_scalar(pool_u[i // 2][:, 16 + (i % 2) * BANK:16 + (i % 2 + 1) * BANK], ps[:], pool_s[:, i // 2:i // 2 + 1], None,
                                      ALU.mult).then_inc(aux_free, 1)
                for i in range(4):
                    ps = bank("u", hf, i)
                    dve.tensor_copy(u_sb[:, 4 * i:4 * i + 4, :].rearrange("p g c -> p (g c)"), ps[:]
                                    ).then_inc(aux_free, 1)
                if hf == 0:
                    dve.wait_ge(toep_set, 16 * TAU)
                    dve.memset(xs[:, :, 0:1], 0.0)
                    link(dve.memset(xw[:, :, 0:1], 0.0))
                for i in range(4):
                    ps = bank("v", hf, i)
                    src = ps[:].rearrange("p (g c) -> p g c", g=4)
                    g4 = slice(4 * i, 4 * i + 4)
                    dve.tensor_copy(xs[:, g4, 1:CHUNKS + 1], src)
                    dve.tensor_copy(xw[0:64, g4, 1:CHUNKS + 1], src[64:P])
                    dve.tensor_copy(xw[64:P, g4, 1:CHUNKS + 1], src[0:64]).then_inc(aux_free, 1)
                dve.wait_ge(aux_free, uses["v", hf] + 4)
                dve.nop().then_inc(v_ready, 1)
                if hf == 1:
                    dve.tensor_scalar(zf_m[:], zf[:], 0.0, None, ALU.min)
                    link(dve.scalar_tensor_tensor(zf[:], zf[:], -1.0, zf[:], ALU.mult, ALU.max))
                    dve.nop().then_inc(f_arg, 1)
                with dve.Fori(0, T_QKV // 2 - 1) as i:
                    for u in range(2):
                        dve.wait_ge(tile_done, i * 2 + (n0 + T_ZA + T_SIL + u + 1))
                        dve.wait_ge(z_stored[u], i * 16 + 8 * (hf * (T_SIL + T_QKV) + T_SIL))
                        dve.tensor_scalar(zout[u][:], tile_ps[u][:], bias[:, bass.ds(i * 2 + (T_ZA + T_SIL + u), 1)],
                                          None, ALU.add).then_inc(tile_out, 1)
                        split_w(u, i * 2 + (n0 + T_ZA + T_SIL + u + 2))
                for u in range(2):
                    n = n0 + T_HALF - 2 + u
                    dve.wait_ge(tile_done, n + 1)
                    dve.wait_ge(z_stored[u], 8 * (hf + 1) * (T_SIL + T_QKV) - 16)
                    dve.tensor_scalar(zout[u][:], tile_ps[u][:], bias[:, T_HALF - 2 + u:T_HALF - 1 + u],
                                      None, ALU.add).then_inc(tile_out, 1)
                    if hf == 0:
                        split_w(u, n + 2)
                if hf == 1:
                    dve.wait_ge(f_ln, 1)
                    dve.tensor_tensor(zf_m[:], zf_m[:], zf[:], ALU.subtract).then_inc(f_arg, 1)
                    for i in range(4):
                        ps = bank("forget", 1, i)
                        dst = fcum[:, (i // 2) * HALF:(i // 2 + 1) * HALF].rearrange("p (c t) -> p t c", t=TAU)
                        ins = dve.tensor_copy(dst[:, 4 * (i % 2):4 * (i % 2) + 4, :],
                                              ps[0:HEADS, :].rearrange("p (t c) -> p t c", t=4)).then_inc(aux_free, 1)
                    dve.wait_ge(aux_free, uses["y", 1])
                    dve.tensor_tensor_scan(fcum, one[:].broadcast_to([HEADS, S]), fcum, 0.0, ALU.mult,
                                           ALU.add).then_inc(f_done, 1)
                for i in range(4):
                    ps = bank("y", hf, i)
                    dst = zs_y[:, :, 64 * i:64 * i + 64].rearrange("p t (g h) -> p g t h", g=4)
                    dve.tensor_copy(dst, ps[:].rearrange("p (g t h) -> p g t h", g=4, t=TAU)).then_inc(aux_free, 1)
                if hf == 0:
                    dve.tensor_copy(xs[:, :, 0], xs[:, :, CHUNKS])
                    dve.tensor_copy(xw[:, :, 0], xw[:, :, CHUNKS])
                    split_x(1, range(KT // 2))
                for i in range(4):
                    ps = bank("yT", hf, i)
                    dst = yT[:, i // 2, :].rearrange("p (c t) -> p t c", t=TAU)[:, 4 * (i % 2):4 * (i % 2) + 4, :]
                    dve.tensor_copy(dst, ps[:].rearrange("p (t c) -> p t c", t=4)).then_inc(yT_in, 1)
                    dve.wait_ge(yT_in, 4 * hf + i + 1)
                    dve.nop().then_inc(aux_free, 1)
                for i in range(4):
                    ps = bank("glu", hf, i)
                    dve.tensor_scalar(glu_v[:, i // 2, (i % 2) * BANK:(i % 2 + 1) * BANK], ps[:],
                                      glu_b[:, i // 2:i // 2 + 1], None, ALU.add).then_inc(glu_in, 1)
                    dve.wait_ge(glu_in, 4 * hf + i + 1)
                    dve.nop().then_inc(aux_free, 1)
                for e in range(2):
                    dve.wait_ge(glu_sig, 2 * hf + e + 1)
                    dve.tensor_tensor(glu_v[:, e, :], glu_v[:, e, :], yT[:, e, :], ALU.mult).then_inc(glu_out, 1)
                if hf == 0:
                    split_x(1, range(KT // 2, KT))

        @block.tensor
        def _(pe):
            def open_bank(name, hf, i):
                n = uses[name, hf] + i
                if n >= 4:
                    pe.wait_ge(aux_free, n - 3)
                return aux_ps[n % 4]

            def project(par, n, hf=None):
                pe.wait_ge(w_split, n + 1)
                for k in range(KT):
                    if hf is not None:
                        pe.wait_ge(x_split, hf * KT + k + 1)
                    for j, (w, x) in enumerate(((w_hi, x_hi), (w_lo, x_hi), (w_hi, x_lo))):
                        for c in range(NCH):
                            last = pe.matmul(tile_ps[par][:, c * BANK:(c + 1) * BANK], w[par][:, k, :],
                                             x[:, k, c * BANK:(c + 1) * BANK], start=(k == 0 and j == 0),
                                             stop=(k == KT - 1 and j == 2))
                last.then_inc(tile_done, 1)

            for hf in range(2):
                n0 = hf * T_HALF
                for i in range(T_ZA):
                    if hf == 1:
                        pe.wait_ge(tile_out, n0 + i - 1)
                    project(i, n0 + i, hf if i == 0 else None)
                if hf == 0:
                    pe.wait_ge(cf_split, 1)
                for t in range(TAU):
                    ps = open_bank("cf", hf, t)
                    for k in range(KT):
                        for j, (x, w) in enumerate(((x_hi, wcf_hi), (x_hi, wcf_lo), (x_lo, wcf_hi))):
                            last = pe.matmul(ps[:, 0:ZCF], x[:, k, t:HALF:TAU], w[:, k, :],
                                             start=(k == 0 and j == 0), stop=(k == KT - 1 and j == 2))
                    last.then_inc(aux_full, 1)
                with pe.Fori(0, T_SIL // 2) as i:
                    for u in range(2):
                        pe.wait_ge(tile_out, i * 2 + (n0 + T_ZA + u - 1))
                        project(u, i * 2 + (n0 + T_ZA + u))
                if hf == 0:
                    pe.wait_ge(in_table, 1)
                    for i in range(4):
                        ps = open_bank("in_table", 0, i)
                        for g in range(4):
                            last = pe.transpose(ps[:, g * P:(g + 1) * P], xs[:, 4 * i + g, 0:P], ident[:])
                        last.then_inc(aux_full, 1)
                    pe.wait_ge(out_table, 1)
                    for i in range(4):
                        ps = open_bank("kern", 0, i)
                        for g in range(4):
                            last = pe.matmul(ps[0:GC, g * P:(g + 1) * P], bb[:, 4 * i + g, :],
                                             m_out[:, 4 * i + g, 0:TAU, :], start=True, stop=True)
                        last.then_inc(aux_full, 1)
                    pe.wait_ge(pool_w_in, 64)
                pe.wait_ge(pooled, hf + 1)
                for i in range(4):
                    ps = open_bank("pool", hf, i)
                    pe.matmul(ps[:], pool_w[:, i // 2, :], pool_u[i // 2][:, 16 + (i % 2) * BANK:16 + (i % 2 + 1) * BANK],
                              start=True, stop=True).then_inc(aux_full, 1)
                for i in range(4):
                    ps = open_bank("u", hf, i)
                    for g in range(4):
                        last = pe.transpose(ps[:, g * P:(g + 1) * P],
                                            zs[:, 4 * i + g].rearrange("p t h -> p (t h)"), ident[:])
                    last.then_inc(aux_full, 1)
                pe.wait_ge(aux_free, uses["u", hf] + 4)
                for i in range(4):
                    ps = open_bank("v", hf, i)
                    for g in range(4):
                        last = pe.matmul(ps[:, g * P:(g + 1) * P], m_in[:, 4 * i + g, :], u_sb[:, 4 * i + g, :],
                                         start=True, stop=True)
                    last.then_inc(aux_full, 1)
                with pe.Fori(0, T_QKV // 2) as i:
                    for u in range(2):
                        pe.wait_ge(tile_out, i * 2 + (n0 + T_ZA + T_SIL + u - 1))
                        project(u, i * 2 + (n0 + T_ZA + T_SIL + u))
                if hf == 1:
                    pe.wait_ge(f_arg, 2)
                    for i in range(4):
                        ps = open_bank("forget", 1, i)
                        for t in range(4):
                            last = pe.transpose(ps[0:HEADS, t * P:(t + 1) * P], zf_m[:, i // 2, 4 * (i % 2) + t, :],
                                                ident[:])
                        last.then_inc(aux_full, 1)
                pe.wait_ge(scanned, hf + 1)
                pe.wait_ge(toep_set, 16 * TAU)
                for i in range(4):
                    ps = open_bank("y", hf, i)
                    for g in range(4):
                        pe.matmul(ps[:, g * P:(g + 1) * P], xs[:, 4 * i + g, 0:CHUNKS], m_out[:, 4 * i + g, 1:, :],
                                  start=True, stop=False)
                        last = pe.matmul(ps[:, g * P:(g + 1) * P], u_sb[:, 4 * i + g, :], toep[:, 4 * i + g, :],
                                         start=False, stop=True)
                    last.then_inc(aux_full, 1)
                pe.wait_ge(aux_free, uses["y", hf] + 4)
                for i in range(4):
                    ps = open_bank("yT", hf, i)
                    for t in range(4):
                        last = pe.transpose(ps[:, t * P:(t + 1) * P],
                                            zs_y[:, 4 * (i % 2) + t, (i // 2) * P:(i // 2 + 1) * P], ident[:])
                    last.then_inc(aux_full, 1)
                pe.wait_ge(gelu_done, 2 * (hf + 1))
                for i in range(4):
                    ps = open_bank("glu", hf, i)
                    e, c = i // 2, i % 2
                    for j in range(2):
                        last = pe.matmul(ps[:], glu_w[:, j, e * P:(e + 1) * P], yT[:, j, c * BANK:(c + 1) * BANK],
                                         start=(j == 0), stop=(j == 1))
                    last.then_inc(aux_full, 1)

        @block.gpsimd
        def _(pool):
            step = [0]

            def link(ins):
                step[0] += 1
                ins.then_inc(pool_step, 1)
                pool.wait_ge(pool_step, step[0])

            tt, ts = pool.tensor_tensor, pool.tensor_scalar

            def over_h(a, n):
                return a.unsqueeze(3).broadcast_to([P, a.shape[1], n, GC])

            def over_t(a, n):
                return a.unsqueeze(2).broadcast_to([P, a.shape[1], n, GC])

            def tables():
                pool.memset(pw_r[:, :, 0], 1.0)
                pool.memset(pw_i[:, :, 0], 0.0)
                pool.wait_ge(coefs, 1)
                tt_in = (t0, t1, t2, t3)
                for k in range(TAU):
                    if k == 0:
                        ts(pw_r[:, :, 1], abr[:], 1.0, None, ALU.mult)
                        link(ts(pw_i[:, :, 1], abi[:], 1.0, None, ALU.mult))
                        continue
                    r, i = pw_r[:, :, k], pw_i[:, :, k]
                    tt(t0[:], r, abr[:], ALU.mult)
                    tt(t1[:], i, abi[:], ALU.mult)
                    tt(t2[:], r, abi[:], ALU.mult)
                    link(tt(t3[:], i, abr[:], ALU.mult))
                    tt(pw_r[:, :, k + 1], t0[:], t1[:], ALU.subtract)
                    link(tt(pw_i[:, :, k + 1], t2[:], t3[:], ALU.add))
                ts(q_r[:, 0, :], pw_r[:, :, TAU], 1.0, None, ALU.mult)
                link(ts(q_i[:, 0, :], pw_i[:, :, TAU], 1.0, None, ALU.mult))
                for j in range(6):
                    r, i = q_r[:, j, :], q_i[:, j, :]
                    tt(t0[:], r, r, ALU.mult)
                    tt(t1[:], i, i, ALU.mult)
                    link(tt(t2[:], r, i, ALU.mult))
                    tt(q_r[:, j + 1, :], t0[:], t1[:], ALU.subtract)
                    link(tt(q_i[:, j + 1, :], t2[:], t2[:], ALU.add))
                ts(q_s[:], q_i[:], sgn[:, 0:1], None, ALU.mult)
                for t in range(TAU):
                    ts(rv_r[:, :, t], pw_r[:, :, TAU - 1 - t], 1.0, None, ALU.mult)
                    ts(rv_i[:, :, t], pw_i[:, :, TAU - 1 - t], sgn[:, 0:1], None, ALU.mult)
                ts(po_r[:], pw_r[:], sgn[:, 1:2], None, ALU.mult)
                ts(po_i[:], pw_i[:], -1.0, None, ALU.mult)
                link(ts(t0[:], ci[:], sgn[:, 0:1], None, ALU.mult))
                r = cr[:].unsqueeze(2).broadcast_to([P, GROUPS, GC])
                i = t0[:].unsqueeze(2).broadcast_to([P, GROUPS, GC])
                h0, h1 = xw[:, :, 0:GC], xw[:, :, GC:2 * GC]
                tt(bb[:], r, bx[:], ALU.mult)
                tt(bw[:], r, by[:], ALU.mult)
                tt(h0, i, by[:], ALU.mult)
                link(tt(h1, i, bx[:], ALU.mult))
                tt(bb[:], bb[:], h0, ALU.add)
                link(tt(bw[:], bw[:], h1, ALU.subtract))
                win = xs[:, :, 0:P].rearrange("p g (t h) -> p g t h", t=TAU)
                part = xw[:, :, 0:P].rearrange("p g (t h) -> p g t h", t=TAU)
                tt(win, over_h(rv_r[:], TAU), over_t(bb[:], TAU), ALU.mult)
                link(tt(part, over_h(rv_i[:], TAU), over_t(bw[:], TAU), ALU.mult))
                tt(win, win, part, ALU.add).then_inc(in_table, 1)
                pool.wait_ge(in_table, 1)
                for g in range(0, GROUPS, 8):
                    g8 = slice(g, g + 8)
                    part = xw[:].rearrange("p g c -> p (g c)")[:, 0:8 * 9 * GC].rearrange(
                        "p (g t h) -> p g t h", g=8, t=TAU + 1)
                    tt(m_out[:, g8], over_h(po_r[:, g8], TAU + 1), over_t(cx[:, g8], TAU + 1), ALU.mult)
                    link(tt(part, over_h(po_i[:, g8], TAU + 1), over_t(cy[:, g8], TAU + 1), ALU.mult))
                    link(tt(m_out[:, g8], m_out[:, g8], part, ALU.add))
                pool.nop().then_inc(out_table, 1)

            def combine(j, dst, src, n):
                t = [zs_flat[:, 0:GROUPS * n], zs_flat[:, 1024:1024 + GROUPS * n],
                     tmp[:, 0, 0:GROUPS * n], tmp[:, 1, 0:GROUPS * n]]
                t = [a.rearrange("p (g n) -> p g n", g=GROUPS) for a in t]
                r = q_r[:, j, :].unsqueeze(2).broadcast_to([P, GROUPS, n])
                i = q_s[:, j, :].unsqueeze(2).broadcast_to([P, GROUPS, n])
                tt(t[0], xs[:, :, src], r, ALU.mult)
                tt(t[1], xw[:, :, src], i, ALU.mult)
                tt(t[2], xw[:, :, src], r, ALU.mult)
                link(tt(t[3], xs[:, :, src], i, ALU.mult))
                tt(xs[:, :, dst], xs[:, :, dst], t[0], ALU.add)
                link(tt(xw[:, :, dst], xw[:, :, dst], t[2], ALU.add))
                tt(xs[:, :, dst], xs[:, :, dst], t[1], ALU.add)
                link(tt(xw[:, :, dst], xw[:, :, dst], t[3], ALU.subtract))

            def store_mix(row0, now, src, done):
                pool.dma_start(scr["mixT"][row0:row0 + P, now], src).then_inc(done, 16)

            for rows, c, v in ((slice(0, 64), 0, -1.0), (slice(64, P), 0, 1.0), (slice(0, 64), 1, 1.0),
                               (slice(64, P), 1, -1.0)):
                link(pool.memset(sgn[rows, c:c + 1], v))
            pool.memset(toep[:], 0.0).then_inc(toep_zero, 1)
            pool.memset(pool_w[:], 0.0).then_inc(pool_w_zero, 1)
            pool.wait_ge(pool_w_zero, 1)
            for w in range(4):
                a = 64 * (w % 2)
                pool.dma_start(pool_w[a:a + 64, w // 2, a:a + 64], io["pool_w"][w]).then_inc(pool_w_in, 16)
            for hf in range(2):
                now = slice(hf * HALF, (hf + 1) * HALF)
                if hf == 0:
                    tables()
                    pool.wait_ge(kern_ready, 1)
                    pool.wait_ge(toep_zero, 1)
                    for s in range(TAU):
                        pool.dma_start(toep[GC * s:GC * (s + 1), :, GC * s:P],
                                       kern[:, :, 0:P - GC * s]).then_inc(toep_set, 16)
                pool.wait_ge(aux_free, uses["pool", hf] + 4)
                for i in range(2):
                    store_mix(i * P, now, pool_u[i][:, 16:], pool_stored)
                pool.wait_ge(v_ready, hf + 1)
                combine(0, slice(1, 2), slice(0, 1), 1)
                for j in range(7):
                    d = 1 << j
                    combine(j, slice(2 * d, CHUNKS + 1, 2 * d), slice(d, CHUNKS + 1 - d, 2 * d), CHUNKS // (2 * d))
                for j in reversed(range(6)):
                    d = 1 << j
                    n = CHUNKS // (2 * d) - 1
                    combine(j, slice(3 * d, 3 * d + 2 * d * (n - 1) + 1, 2 * d),
                            slice(2 * d, 2 * d + 2 * d * (n - 1) + 1, 2 * d), n)
                pool.nop().then_inc(scanned, 1)
                if hf == 1:
                    pool.wait_ge(f_done, 1)
                    pool.dma_start(scr["fcum"], fcum).then_inc(f_stored, 16)
                for e in range(2):
                    pool.wait_ge(glu_out, 2 * hf + e + 1)
                    store_mix(D_C + D_B + e * P, now, glu_v[:, e, :], glu_stored)
            pool.wait_ge(pool_stored, 64)
            pool.wait_ge(glu_stored, 64)
            pool.wait_ge(f_stored, 16)


def fill_plan():
    per_piece = 3 * KT
    total = G_TILES * NCH * per_piece
    steps = [(t, j) for t in range(Q_TILES) for j in range(-(-(t + 1) // 4))]
    slots = ["start", *steps, "end"]
    counts = {s: FILL_BETWEEN for s in steps}
    counts.update({"start": FILL_START, "end": FILL_END})
    rest = total - sum(counts[s] for s in slots if s == "start" or s == "end" or s[1])
    for t in range(Q_TILES):
        counts[t, 0] = rest * (t + 1) // Q_TILES - rest * t // Q_TILES
    ends, splits, done = {s: [] for s in slots}, {s: [] for s in slots}, 0
    splits["start"].append(1)
    for n, s in enumerate(slots):
        before, done = done, done + counts[s]
        for piece in range(before // per_piece, done // per_piece):
            ends[s].append(piece)
            if piece % NCH == NCH - 1 and piece // NCH + 2 <= G_TILES:
                later = next(a for a in slots[n + 1:] if a == "end" or a[1] == 0)
                splits[later].append(piece // NCH + 2)
    assert done == total
    return counts, ends, splits


Q_TILES = S // P
PHASE_HEADS = HEADS // 2
G_TILES = T_GATE // PHASE_HEADS
FILL_START, FILL_END, FILL_BETWEEN = 36, 36, 3
S_PIECES = sum(-(-(t + 1) // 4) for t in range(Q_TILES))
PT_USES = 2 + S_PIECES


def stage_attend(nc, io, scr, ident, ident_b, mask, x_hi, x_lo, x_raw):
    fill_counts, fill_ends, w_splits = fill_plan()

    with ExitStack() as ctx:
        def sb(name, shape, dt=F32):
            return ctx.enter_context(nc.sbuf_tensor(name, shape, dt))

        def sem(name):
            return ctx.enter_context(nc.semaphore(name))

        gw_hi = [sb(f"gw_hi{i}", [P, KT, P], F32R) for i in range(2)]
        gw_lo, gw_raw = zip(*(low_with_raw(nc, ctx, f"gw_lo{i}", [P, KT, P]) for i in range(2)))
        g_bias = sb("g_bias", [P, T_GATE])
        g_out = [sb(f"g_out{i}", [P, BANK]) for i in range(NCH)]
        k_hh = sb("k_hh", [P, S], F32R)
        k_ll = sb("k_ll", [P, S], F32R)
        q_st = sb("q_st", [P, S], F32R)
        q_tmp = sb("q_tmp", [P, S], F32R)
        vT = sb("vT", [HD, S])
        v_st = sb("v_st", [P, Q_TILES, 2 * HD], F32R)
        f_row = sb("f_row", [P, S])
        s_sb = [sb(f"s_sb{i}", [P, S]) for i in range(2)]
        mx = [sb(f"mx{i}", [P, 4]) for i in range(2)]
        neg_max = [sb(f"neg_max{i}", [P, 1]) for i in range(2)]
        row_sum = sb("row_sum", [P, Q_TILES])
        row_inv = sb("row_inv", [P, Q_TILES])
        pt_hi = sb("pt_hi", [P, Q_TILES, 2 * P], F32R)
        pt_lo = sb("pt_lo", [P, Q_TILES, 2 * P], F32R)
        o_low = sb("o_low", [HD, 2 * P])
        y_out = [sb(f"y_out{i}", [HD, 2 * P]) for i in range(2)]

        s_ps = [ctx.enter_context(nc.psum_tensor(f"s_ps{i}", [P, BANK], F32)) for i in range(3)]
        t_ps = [ctx.enter_context(nc.psum_tensor(f"t_ps{i}", [P, BANK], F32)) for i in range(2)]
        o_ps = ctx.enter_context(nc.psum_tensor("o_ps", [P, 2, 2 * P], F32))
        g_ps = [ctx.enter_context(nc.psum_tensor(f"g_ps{i}", [P, BANK], F32)) for i in range(NCH)]

        gw_loaded = [sem(f"gw_loaded{i}") for i in range(2)]
        passed = [sem(f"passed{i}") for i in range(3)]
        g_stored = [sem(f"g_stored{i}") for i in range(NCH)]
        y_stored, y_free = sem("y_stored"), sem("y_free")
        x2_loaded = [sem(f"x2_loaded{k}") for k in range(KT)]
        (x2_hi, x2_split, gb_loaded, gb_half, gw_split_hi, gw_split, g_done, g_ready, kq_loaded, v_loaded, f_loaded, k_hi,
         k_lo, q_hi_tmp, q_hi, q_lo, s_full, s_free, max_ready, p_ready, t_full, t_hi, t_lo, inv_ready, o_full,
         o_low_ready, o_sum, y_ready) = (
            sem(n) for n in (
                "x2_hi", "x2_split", "gb_loaded", "gb_half", "gw_split_hi", "gw_split", "g_done", "g_ready", "kq_loaded",
                "v_loaded", "f_loaded", "k_hi", "k_lo", "q_hi_tmp", "q_hi", "q_lo", "s_full", "s_free", "max_ready",
                "p_ready", "t_full", "t_hi", "t_lo", "inv_ready", "o_full", "o_low_ready", "o_sum", "y_ready"))

        def pieces(t):
            n0 = sum(-(-(a + 1) // 4) for a in range(t))
            keys = (t + 1) * P
            return [(n0 + j, j * BANK, min(BANK, keys - j * BANK)) for j in range(-(-keys // BANK))]

        def pieces_to(t):
            return pieces(t)[-1][0] + 1

        block = ctx.enter_context(nc.Block())

        @block.sync
        def _(sp):
            w_rows = io["w_tiles"].rearrange("m p (k c) -> (m p) k c", c=P)

            def load_w(first_row, par):
                sp.dma_start(gw_raw[par][:], w_rows[bass.ds(first_row, P)]).then_inc(gw_loaded[par], 16)

            def store(row, now, m2, c):
                sp.wait_ge(g_ready, m2 + (NCH + 1))
                sp.dma_start(scr["gateT"][bass.ds(row, P), now + c * BANK:now + (c + 1) * BANK],
                             g_out[c][:]).then_inc(g_stored[c], 16)

            for c in range(NCH):
                sp.sem_inc(g_stored[c], 16)
            sp.dma_start(g_bias[:], io["b_tiles"][:, T_HALF:T_HALF + T_GATE]).then_inc(gb_loaded, 16)
            for u in range(2):
                load_w((T_HALF + u) * P, u)
            for phase in range(2):
                now = (1 - phase) * HALF
                m0 = phase * T_GATE
                if phase == 1:
                    for k in range(KT):
                        sp.dma_start(x_raw[:, k, :],
                                     io["xT"][k * P:(k + 1) * P, 0:HALF]).then_inc(x2_loaded[k], 16)
                with sp.Fori(0, T_GATE // 2 - 1) as i:
                    for u in range(2):
                        for c in range(NCH):
                            store(i * (2 * P) + u * P, now, i * 4 + (m0 * 2 + 2 * u + c), c)
                        sp.wait_ge(g_done, i * 4 + (m0 * 2 + 2 * u + 2))
                        load_w(i * (2 * P) + (T_HALF + u + 2) * P, u)
                for u in range(2):
                    for c in range(NCH):
                        store((T_GATE - 2 + u) * P, now, (m0 + T_GATE - 2 + u) * 2 + c, c)
                    if phase == 0 or u == 0:
                        sp.wait_ge(g_done, (m0 + T_GATE - 1 + u) * 2)
                        load_w((T_HALF + u) * P, u)
            for c in range(NCH):
                sp.wait_ge(g_stored[c], 16 * (2 * T_GATE + 1))

        @block.gpsimd
        def _(pool):
            def load_kq(q_row):
                for half in (slice(0, HD), slice(HD, P)):
                    pool.dma_start(k_ll[half].bitcast(F32), scr["qkvT"][bass.ds(q_row + D_B, HD)]).then_inc(kq_loaded, 16)
                    pool.dma_start(q_st[half].bitcast(F32), scr["qkvT"][bass.ds(q_row, HD)]).then_inc(kq_loaded, 16)
                pool.dma_start(vT[:], scr["qkvT"][bass.ds(q_row + 2 * D_B, HD)]).then_inc(v_loaded, 16)

            def load_f(h):
                pool.dma_start(f_row[:], scr["fcum"][bass.ds(h, 1)].partition_broadcast(P)).then_inc(f_loaded, 16)

            def store_y(h8, row, p):
                pool.wait_ge(y_ready, h8 + (p + 1))
                pool.dma_start(scr["mixT"][bass.ds(row, HD), p * 2 * P:(p + 1) * 2 * P],
                               y_out[p % 2][:]).then_inc(y_stored, 16)
                pool.wait_ge(y_stored, h8 * 16 + 16 * (p + 1))
                pool.sem_inc(y_free, 1)

            pool.sem_inc(y_free, 2)
            load_kq(0)
            load_f(0)
            with pool.Fori(0, HEADS - 1) as h:
                for p in range(7):
                    store_y(h * 8, h * HD + 2 * P, p)
                pool.wait_ge(s_full, h * S_PIECES + S_PIECES)
                load_kq(h * HD + HD)
                pool.wait_ge(s_free, h * S_PIECES + S_PIECES)
                load_f(h + 1)
                store_y(h * 8, h * HD + 2 * P, 7)
            for p in range(8):
                store_y((HEADS - 1) * 8, (HEADS - 1) * HD + 2 * P, p)

        def phases(eng, before, body):
            for phase in range(2):
                before(phase)
                with eng.Fori(0, PHASE_HEADS) as i:
                    body(lambda k, c: i * k + (c + phase * PHASE_HEADS * k), lambda k, c: i * k + c)

        @block.scalar
        def _(act):
            def split_w(at, j):
                act.wait_ge(gw_loaded[j % 2], at(G_TILES * 8, 16 * (j // 2 + 1)))
                act.activation(gw_hi[j % 2][:], gw_raw[j % 2][:], ACT.Copy).then_inc(gw_split_hi, 1)

            def gates(at, in_phase, slot):
                for j in w_splits[slot]:
                    split_w(at, j)
                for piece in fill_ends[slot]:
                    j, c = divmod(piece, NCH)
                    act.wait_ge(g_done, at(G_TILES * NCH, piece + 1))
                    act.wait_ge(g_stored[c], at(G_TILES * 16, 16 * (j + 1)))
                    act.sem_inc(passed[0])
                    act.activation(g_out[c][:], g_ps[c][:], ACT.Tanh, scale=0.5,
                                   bias=g_bias[:, bass.ds(in_phase(G_TILES, j), 1)]).then_inc(g_ready, 1)

            def low_rows(at, p):
                act.wait_ge(o_full, at(8, p + 1))
                act.activation(o_low[:], o_ps[HD:P, 0, :], ACT.Copy).then_inc(o_low_ready, 1)

            def before(phase):
                if phase == 0:
                    act.wait_ge(gb_loaded, 16)
                    act.activation(g_bias[:], g_bias[:], ACT.Copy, scale=0.5).then_inc(gb_half, 1)
                    act.wait_ge(gb_half, 1)
                    act.wait_ge(gw_loaded[0], 16)
                    act.activation(gw_hi[0][:], gw_raw[0][:], ACT.Copy).then_inc(gw_split_hi, 1)
                else:
                    for k in range(KT):
                        act.wait_ge(x2_loaded[k], 16)
                        act.activation(x_hi[:, k, :], x_raw[:, k, :], ACT.Copy).then_inc(x2_hi, 1)

            def body(at, in_phase):
                act.wait_ge(kq_loaded, at(64, 64))
                act.activation(k_hh[:], k_ll[:].bitcast(F32), ACT.Copy).then_inc(k_hi, 1)
                act.activation(q_tmp[HD:P], q_st[HD:P].bitcast(F32), ACT.Copy, scale=HD ** -0.5).then_inc(q_hi_tmp, 1)
                act.activation(q_st[0:HD], q_st[0:HD].bitcast(F32), ACT.Copy, scale=HD ** -0.5).then_inc(q_hi, 1)
                for b in range(2):
                    act.wait_ge(t_full, at(PT_USES, b + 1))
                    act.activation(v_st[:, 8 * b:8 * b + 8, 0:HD], t_ps[b][:].rearrange("p (t d) -> p t d", t=8),
                                   ACT.Copy).then_inc(t_hi, 1)
                gates(at, in_phase, "start")
                for t in range(Q_TILES):
                    act.wait_ge(max_ready, at(Q_TILES, t + 1))
                    row = s_sb[t % 2][:, 0:(t + 1) * P]
                    act.activation(row, row, ACT.Exp, bias=neg_max[t % 2][:],
                                   accum_out=row_sum[:, t:t + 1]).then_inc(p_ready, 1)
                    gates(at, in_phase, (t, 0))
                    if t % 2 == 0 and t >= 2:
                        low_rows(at, t // 2 - 1)
                    for j, (n, k0, keys) in enumerate(pieces(t)):
                        if j:
                            gates(at, in_phase, (t, j))
                        act.wait_ge(t_full, at(PT_USES, n + 3))
                        act.activation(pt_hi[:, k0 // P:(k0 + keys) // P, (t % 2) * P:(t % 2 + 1) * P],
                                       t_ps[n % 2][:, 0:keys].rearrange("p (k q) -> p k q", q=P),
                                       ACT.Copy).then_inc(t_hi, 1)
                gates(at, in_phase, "end")
                low_rows(at, 7)

            phases(act, before, body)

        @block.vector
        def _(dve):
            def split_w(at, j):
                dve.wait_ge(gw_split_hi, at(G_TILES, j + 1))
                dve.tensor_tensor(gw_lo[j % 2][:], gw_raw[j % 2][:], gw_hi[j % 2][:].bitcast(F32),
                                  ALU.subtract).then_inc(gw_split, 1)

            def logits(at, t):
                for j, (n, k0, keys) in enumerate(pieces(t)):
                    dve.wait_ge(s_full, at(S_PIECES, n + 1))
                    if t >= 2 and j == 0:
                        dve.wait_ge(t_full, at(PT_USES, pieces_to(t - 2) + 2))
                    dve.sem_inc(passed[1])
                    dve.tensor_tensor_reduce(s_sb[t % 2][:, k0:k0 + keys], s_ps[n % 3][:, 0:keys],
                                             f_row[:, k0:k0 + keys], 1.0, -3e38, ALU.subtract, ALU.max,
                                             mx[t % 2][:, j:j + 1]).then_inc(s_free, 1)
                dve.wait_ge(s_free, at(S_PIECES, pieces_to(t)))
                dve.tensor_reduce(neg_max[t % 2][:], mx[t % 2][:, 0:len(pieces(t))], AX_X, ALU.max,
                                  negate=True).then_inc(max_ready, 1)

            def output(at, p):
                dve.wait_ge(o_low_ready, at(8, p + 1))
                dve.wait_ge(y_free, at(8, p + 1))
                y = y_out[p % 2]
                dve.tensor_tensor(y[:], o_ps[0:HD, 0, :], o_low[:], ALU.add).then_inc(o_sum, 1)
                dve.wait_ge(o_sum, at(8, p + 1))
                dve.tensor_tensor(y[:], y[:], o_ps[0:HD, 1, :], ALU.mult).then_inc(y_ready, 1)

            def before(phase):
                if phase == 0:
                    dve.wait_ge(gw_split_hi, 1)
                    dve.tensor_tensor(gw_lo[0][:], gw_raw[0][:], gw_hi[0][:].bitcast(F32),
                                      ALU.subtract).then_inc(gw_split, 1)
                else:
                    for k in range(KT):
                        dve.wait_ge(x2_hi, k + 1)
                        dve.tensor_tensor(x_lo[:, k, :], x_raw[:, k, :], x_hi[:, k, :].bitcast(F32),
                                          ALU.subtract).then_inc(x2_split, 1)

            def body(at, in_phase):
                dve.wait_ge(k_hi, at(1, 1))
                dve.tensor_tensor(k_ll[:], k_ll[:].bitcast(F32), k_hh[:].bitcast(F32),
                                  ALU.subtract).then_inc(k_lo, 1)
                dve.wait_ge(q_hi_tmp, at(1, 1))
                dve.scalar_tensor_tensor(q_st[HD:P], q_st[HD:P].bitcast(F32), HD ** -0.5, q_tmp[HD:P].bitcast(F32),
                                         ALU.mult, ALU.subtract).then_inc(q_lo, 1)
                for b in range(2):
                    dve.wait_ge(t_hi, at(PT_USES, b + 1))
                    v8 = v_st[:, 8 * b:8 * b + 8, :]
                    dve.tensor_tensor(v8[:, :, HD:], t_ps[b][:].rearrange("p (t d) -> p t d", t=8),
                                      v8[:, :, 0:HD].bitcast(F32), ALU.subtract).then_inc(t_lo, 1)
                for j in w_splits["start"]:
                    split_w(at, j)
                dve.wait_ge(f_loaded, at(16, 16))
                logits(at, 0)
                for t in range(Q_TILES):
                    if t + 1 < Q_TILES:
                        logits(at, t + 1)
                    for j in w_splits[t, 0]:
                        split_w(at, j)
                    if t % 2 == 0 and t >= 2:
                        output(at, t // 2 - 1)
                    if t % 2 == 1:
                        dve.wait_ge(p_ready, at(Q_TILES, t + 1))
                        dve.reciprocal(row_inv[:, t - 1:t + 1], row_sum[:, t - 1:t + 1]).then_inc(inv_ready, 1)
                    for n, k0, keys in pieces(t):
                        dve.wait_ge(t_hi, at(PT_USES, n + 3))
                        part = (slice(None), slice(k0 // P, (k0 + keys) // P), slice((t % 2) * P, (t % 2 + 1) * P))
                        dve.tensor_tensor(pt_lo[part], t_ps[n % 2][:, 0:keys].rearrange("p (k q) -> p k q", q=P),
                                          pt_hi[part].bitcast(F32), ALU.subtract).then_inc(t_lo, 1)
                for j in w_splits["end"]:
                    split_w(at, j)
                output(at, 7)

            phases(dve, before, body)

        @block.tensor
        def _(pe):
            def queries(at, t):
                for n, k0, keys in pieces(t):
                    if n >= 3:
                        pe.wait_ge(s_free, at(S_PIECES, n - 2))
                    ps = s_ps[n % 3][:, 0:keys]
                    last_piece = k0 + keys == (t + 1) * P
                    pe.matmul(ps, q_st[:, t * P:(t + 1) * P], k_hh[:, k0:k0 + keys], start=True, stop=False)
                    last = pe.matmul(ps, q_st[:, t * P:(t + 1) * P], k_ll[:, k0:k0 + keys], start=False,
                                     stop=not last_piece)
                    if last_piece:
                        last = pe.matmul(ps[:, keys - P:keys], ident_b[:], mask[:], start=False, stop=True)
                    last.then_inc(s_full, 1)

            def turn(at, t, fill):
                pe.wait_ge(p_ready, at(Q_TILES, t + 1))
                for j, (n, k0, keys) in enumerate(pieces(t)):
                    if j:
                        fill((t, j))
                    pe.wait_ge(t_lo, at(PT_USES, n + 1))
                    for a in range(keys // P):
                        last = pe.transpose(t_ps[n % 2][:, a * P:(a + 1) * P],
                                            s_sb[t % 2][:, k0 + a * P:k0 + (a + 1) * P], ident[:])
                    last.then_inc(t_full, 1)

            def values(at, p):
                pe.wait_ge(t_lo, at(PT_USES, pieces_to(2 * p + 1) + 2))
                if p:
                    pe.wait_ge(y_ready, at(8, p))
                last_key = 2 * p + 1
                for k in range(last_key + 1):
                    q = slice(P, 2 * P) if k == last_key else slice(0, 2 * P)
                    for j, pt in enumerate((pt_hi, pt_lo)):
                        pe.matmul(o_ps[:, 0, q], v_st[:, k, :], pt[:, k, q], start=(k == 0 and j == 0),
                                  stop=(k == last_key and j == 1))
                pe.wait_ge(inv_ready, at(8, p + 1))
                pe.sem_inc(passed[2])
                for a in range(2):
                    last = pe.transpose(o_ps[0:HD, 1, a * P:(a + 1) * P],
                                        row_inv[:, 2 * p + a:2 * p + a + 1].broadcast_to([P, HD]), ident[:])
                last.then_inc(o_full, 1)

            pe.sem_inc(g_ready, NCH)
            for phase in range(2):
                with pe.Fori(0, PHASE_HEADS) as i:
                    def at(k, c):
                        return i * k + (c + phase * PHASE_HEADS * k)

                    filled = [0]

                    def fill(slot):
                        for _ in range(fill_counts[slot]):
                            piece, r = divmod(filled[0], 3 * KT)
                            j, c = divmod(piece, NCH)
                            k, a = divmod(r, 3)
                            filled[0] += 1
                            if r == 0:
                                if c == 0:
                                    pe.wait_ge(gw_split, at(G_TILES, j + 1))
                                pe.wait_ge(g_ready, at(G_TILES * NCH, piece + 1))
                                if phase == 1 and piece == 0:
                                    pe.wait_ge(x2_split, KT)
                            w, x = ((gw_hi, x_hi), (gw_lo, x_hi), (gw_hi, x_lo))[a]
                            mm = pe.matmul(g_ps[c][:], w[j % 2][:, k, :], x[:, k, c * BANK:(c + 1) * BANK],
                                           start=(r == 0), stop=(r == 3 * KT - 1))
                            if r == 3 * KT - 1:
                                mm.then_inc(g_done, 1)

                    pe.wait_ge(v_loaded, at(16, 16))
                    pe.sem_inc(passed[2])
                    for b in range(2):
                        for t in range(8):
                            k = 8 * b + t
                            last = pe.transpose(t_ps[b][:, t * HD:(t + 1) * HD], vT[:, k * P:(k + 1) * P],
                                                ident[0:HD, 0:HD])
                        last.then_inc(t_full, 1)
                    fill("start")
                    pe.wait_ge(k_lo, at(1, 1))
                    pe.wait_ge(q_hi, at(1, 1))
                    pe.wait_ge(q_lo, at(1, 1))
                    queries(at, 0)
                    for t in range(Q_TILES):
                        if t + 1 < Q_TILES:
                            queries(at, t + 1)
                        fill((t, 0))
                        if t % 2 == 0 and t >= 2:
                            values(at, t // 2 - 1)
                        turn(at, t, fill)
                    fill("end")
                    values(at, 7)


BLOCK = 2 * P
BLOCKS = S // BLOCK
RING = 4
BRANCH_K = ((0, 2), (2, 6), (6, 8))


def stage_merge(nc, io, scr, out):
    with ExitStack() as ctx:
        def sb(name, shape, dt=F32):
            return ctx.enter_context(nc.sbuf_tensor(name, shape, dt))

        def sem(name):
            return ctx.enter_context(nc.semaphore(name))

        wu_hi, wo_hi = sb("wu_hi", [P, KT, KT, P], F32R), sb("wo_hi", [P, KT, D], F32R)
        wu_lo, wu_raw = low_with_raw(nc, ctx, "wu_lo", [P, KT, KT, P])
        wo_lo, wo_raw = low_with_raw(nc, ctx, "wo_lo", [P, KT, D])
        mix = [sb(f"mix{g}", [P, 4, BLOCK]) for g in range(2)]
        sil = [sb(f"sil{g}", [P, 4, BLOCK]) for g in range(2)]
        y_hi, y_lo = sb("y_hi", [P, KT, BLOCK], F32R), sb("y_lo", [P, KT, BLOCK], F32R)
        m_hi, m_lo = sb("m_hi", [P, KT, BLOCK], F32R), sb("m_lo", [P, KT, BLOCK], F32R)
        gate = [sb(f"gate{i}", [P, 3, BLOCK]) for i in range(RING)]
        x_t = [sb(f"x_t{m}", [P, D]) for m in range(2)]
        ln_g, ln_b = sb("ln_g", [P, D]), sb("ln_b", [P, D])
        stats = [sb(f"stats{m}", [P, 2, 6]) for m in range(2)]
        mean_var = [sb(f"mean_var{m}", [P, 2]) for m in range(2)]
        fix = [sb(f"fix{m}", [P, 1]) for m in range(2)]
        rstd = [sb(f"rstd{m}", [P, 1]) for m in range(2)]

        u_ps = [ctx.enter_context(nc.psum_tensor(f"u_ps{i}", [P, 4, BLOCK], F32)) for i in range(2)]
        h_ps = [ctx.enter_context(nc.psum_tensor(f"h_ps{m}", [P, D], F32)) for m in range(2)]

        wu_loaded = [sem(f"wu_loaded{i}") for i in range(KT)]
        wo_loaded = [sem(f"wo_loaded{i}") for i in range(KT)]
        gate_loaded = [sem(f"gate_loaded{i}") for i in range(RING)]
        mix_loaded = [sem(f"mix_loaded{g}") for g in range(2)]
        xt_loaded = [sem(f"xt_loaded{m}") for m in range(2)]
        out_stored = [sem(f"out_stored{m}") for m in range(2)]
        (ln_loaded, passed, wu_high, wu_split, wo_high, wo_split, prod, y_high, y_split, lifted, weighted, part_sum, merged,
         m_high, m_split, h_full, h_sum, h_stats, h_mean, h_var, h_root, h_rstd, h_norm, h_scaled, h_out) = (
            sem(n) for n in (
                "ln_loaded", "passed", "wu_high", "wu_split", "wo_high", "wo_split", "prod", "y_high", "y_split", "lifted",
                "weighted", "part_sum", "merged", "m_high", "m_split", "h_full", "h_sum", "h_stats", "h_mean",
                "h_var", "h_root", "h_rstd", "h_norm", "h_scaled", "h_out"))

        def blocks(eng, body):
            body(0, True, False)
            with eng.Fori(1, BLOCKS - 1) as b:
                body(b, False, False)
            body(BLOCKS - 1, False, True)

        block = ctx.enter_context(nc.Block())

        @block.sync
        def _(sp):
            def load_mix(b):
                for g in range(2):
                    for dst, src in ((mix[g], scr["mixT"]), (sil[g], scr["silT"])):
                        rows = src[g * 4 * P:(g + 1) * 4 * P].rearrange("(k p) t -> p k t", p=P)
                        sp.dma_start(dst[:], rows[:, :, bass.ds(b * BLOCK, BLOCK)]).then_inc(mix_loaded[g], 16)

            gates = scr["gateT"].rearrange("(g d p) t -> d p g t", g=3, p=P)

            def load_gate(b, d):
                sp.dma_start(gate[d % RING][:], gates[d][:, :, bass.ds(b * BLOCK, BLOCK)]
                             ).then_inc(gate_loaded[d % RING], 16)

            def load_wu(i):
                sp.dma_start(wu_raw[:, i].rearrange("p k c -> p (k c)"), io["w_up"][i]
                             ).then_inc(wu_loaded[i], 16)

            load_wu(0)
            load_mix(0)
            load_wu(1)
            for d in range(RING):
                load_gate(0, d)
            for i in range(2, KT):
                load_wu(i)
            for k in range(KT):
                sp.dma_start(wo_raw[:, k, :], io["w_out"][:, k, :]).then_inc(wo_loaded[k], 16)

            def body(b, first, last):
                if not last:
                    sp.wait_ge(y_split, b * 2 + 2)
                    load_mix(b + 1)
                for d in range(KT):
                    sp.wait_ge(m_split, b * KT + (d + 1))
                    if d + RING < KT:
                        load_gate(b, d + RING)
                    elif not last:
                        load_gate(b + 1, d + RING - KT)

            blocks(sp, body)

        @block.scalar
        def _(act):
            def split_wu(i):
                act.wait_ge(wu_loaded[i], 16)
                act.activation(wu_hi[:, i], wu_raw[:, i], ACT.Copy).then_inc(wu_high, 1)

            def split_wo(k):
                act.wait_ge(wo_loaded[k], 16)
                act.activation(wo_hi[:, k], wo_raw[:, k], ACT.Copy).then_inc(wo_high, 1)

            def split_y(b):
                for g in range(2):
                    act.wait_ge(prod, b * 2 + (g + 1))
                    act.activation(y_hi[:, 4 * g:4 * g + 4], mix[g][:], ACT.Copy).then_inc(y_high, 1)

            def root(b, m):
                act.wait_ge(h_var, b * 2 + (m + 1))
                act.activation(rstd[m][:], mean_var[m][:, 1:2], ACT.Sqrt).then_inc(h_root, 1)

            def body(b, first, last):
                for d in range(KT):
                    if first:
                        if d + 2 < KT:
                            split_wu(d + 2)
                        split_wo(d)
                    elif d == 3:
                        root(b - 1, 1)
                    act.wait_ge(merged, b * KT + (d + 1))
                    act.activation(m_hi[:, d], gate[d % RING][:, 0], ACT.Copy, scale=0.5).then_inc(m_high, 1)
                if not last:
                    split_y(b + 1)
                root(b, 0)

            split_wu(0)
            split_y(0)
            split_wu(1)
            blocks(act, body)
            root(BLOCKS - 1, 1)

        @block.vector
        def _(dve):
            def low(dst, src, hi, done):
                dve.tensor_tensor(dst, src, hi.bitcast(F32), ALU.subtract).then_inc(done, 1)

            def split_wu(i):
                dve.wait_ge(wu_high, i + 1)
                low(wu_lo[:, i], wu_raw[:, i], wu_hi[:, i], wu_split)

            def split_wo(k):
                dve.wait_ge(wo_high, k + 1)
                low(wo_lo[:, k], wo_raw[:, k], wo_hi[:, k], wo_split)

            def split_y(b):
                for g in range(2):
                    dve.wait_ge(mix_loaded[g], b * 32 + 32)
                    dve.tensor_tensor(mix[g][:], mix[g][:], sil[g][:], ALU.mult).then_inc(prod, 1)
                for g in range(2):
                    dve.wait_ge(y_high, b * 2 + (g + 1))
                    low(y_lo[:, 4 * g:4 * g + 4], mix[g][:], y_hi[:, 4 * g:4 * g + 4], y_split)

            def split_m(b, d):
                dve.wait_ge(m_high, b * KT + (d + 1))
                dve.scalar_tensor_tensor(m_lo[:, d], gate[d % RING][:, 0], 0.5, m_hi[:, d].bitcast(F32), ALU.mult,
                                         ALU.subtract).then_inc(m_split, 1)

            def residual(b, m):
                dve.wait_ge(h_full, b * 2 + (m + 1))
                dve.wait_ge(xt_loaded[m], b * 16 + 16)
                dve.scalar_tensor_tensor(x_t[m][:], x_t[m][:], ALPHA, h_ps[m][:], ALU.mult,
                                         ALU.add).then_inc(h_sum, 1)

            def moments(b, m):
                n = m + 1
                dve.wait_ge(h_sum, b * 2 + n)
                for c in range(2):
                    last = dve.bn_stats(stats[m][:, c, :], x_t[m][:, c * BANK:(c + 1) * BANK])
                last.then_inc(h_stats, 1)
                dve.wait_ge(h_stats, b * 2 + n)
                dve.sem_inc(passed)
                dve.bn_aggr(mean_var[m][:], stats[m][:]).then_inc(h_mean, 1)
                dve.wait_ge(h_mean, b * 2 + n)
                var = mean_var[m][:, 1:2]
                dve.tensor_scalar(var, var, EPS, None, ALU.add).then_inc(h_var, 1)

            def normalise(b, m):
                n = m + 1
                var, r, t = mean_var[m][:, 1:2], rstd[m][:], fix[m][:]
                dve.wait_ge(h_root, b * 2 + n)
                dve.reciprocal(r, r).then_inc(h_rstd, 1)
                dve.wait_ge(h_rstd, b * 8 + (4 * m + 1))
                dve.scalar_tensor_tensor(t, r, var, r, ALU.mult, ALU.mult).then_inc(h_rstd, 1)
                dve.wait_ge(h_rstd, b * 8 + (4 * m + 2))
                dve.tensor_scalar(t, t, -0.5, 1.5, ALU.mult, ALU.add).then_inc(h_rstd, 1)
                dve.wait_ge(h_rstd, b * 8 + (4 * m + 3))
                dve.tensor_tensor(r, r, t, ALU.mult).then_inc(h_rstd, 1)
                dve.wait_ge(h_rstd, b * 8 + (4 * m + 4))
                dve.tensor_scalar(x_t[m][:], x_t[m][:], mean_var[m][:, 0:1], rstd[m][:], ALU.subtract,
                                  ALU.mult).then_inc(h_norm, 1)

            def body(b, first, last):
                if not first:
                    residual(b - 1, 1)
                for d in range(KT):
                    if first:
                        if d + 2 < KT:
                            split_wu(d + 2)
                        split_wo(d)
                    dve.wait_ge(lifted, b * KT + (d + 1))
                    dve.wait_ge(gate_loaded[d % RING], b * 32 + 16 * (d // RING + 1))
                    flat = gate[d % RING][:].rearrange("p g t -> p (g t)")
                    dve.scalar_tensor_tensor(flat, flat, 1.0, u_ps[d % 2][:, 0:3].rearrange("p g t -> p (g t)"),
                                             ALU.add, ALU.mult).then_inc(weighted, 1)
                    if not first and d == 3:
                        moments(b - 1, 1)
                    if not first and d == 5:
                        normalise(b - 1, 1)
                    g = gate[d % RING]
                    dve.wait_ge(weighted, b * KT + (d + 1))
                    dve.tensor_tensor(g[:, 0], g[:, 0], g[:, 1], ALU.add).then_inc(part_sum, 1)
                    if d:
                        split_m(b, d - 1)
                    dve.wait_ge(part_sum, b * KT + (d + 1))
                    dve.tensor_tensor(g[:, 0], g[:, 0], g[:, 2], ALU.add).then_inc(merged, 1)
                split_m(b, KT - 1)
                if not last:
                    split_y(b + 1)
                residual(b, 0)
                moments(b, 0)
                normalise(b, 0)

            split_wu(0)
            split_y(0)
            split_wu(1)
            blocks(dve, body)
            residual(BLOCKS - 1, 1)
            moments(BLOCKS - 1, 1)
            normalise(BLOCKS - 1, 1)

        @block.tensor
        def _(pe):
            def body(b, first, last):
                pe.wait_ge(y_split, b * 2 + 2)
                for d in range(KT):
                    if first:
                        pe.wait_ge(wu_split, d + 1)
                    if not first or d >= 2:
                        pe.wait_ge(weighted, b * KT + (d - 1))
                    for n, (k0, k1) in enumerate(BRANCH_K):
                        for k in range(k0, k1):
                            for j, (w, y) in enumerate(((wu_hi, y_hi), (wu_lo, y_hi), (wu_hi, y_lo))):
                                mm = pe.matmul(u_ps[d % 2][:, n, :], w[:, d, k, :], y[:, k, :],
                                               start=(k == k0 and j == 0), stop=(k == k1 - 1 and j == 2))
                    mm.then_inc(lifted, 1)
                if not first:
                    pe.wait_ge(h_sum, b * 2)
                for m in range(2):
                    tok = slice(m * P, (m + 1) * P)
                    for k in range(KT):
                        if m == 0:
                            pe.wait_ge(m_split, b * KT + (k + 1))
                            if first:
                                pe.wait_ge(wo_split, k + 1)
                        for j, (y, w) in enumerate(((m_hi, wo_hi), (m_hi, wo_lo), (m_lo, wo_hi))):
                            for c in range(2):
                                mm = pe.matmul(h_ps[m][:, c * BANK:(c + 1) * BANK], y[:, k, tok],
                                               w[:, k, c * BANK:(c + 1) * BANK], start=(k == 0 and j == 0),
                                               stop=(k == KT - 1 and j == 2))
                    mm.then_inc(h_full, 1)

            blocks(pe, body)

        @block.gpsimd
        def _(pool):
            def load_x(b, m):
                pool.dma_start(x_t[m][:], io["x_tok"][bass.ds(b * BLOCK + m * P, P)]).then_inc(xt_loaded[m], 16)

            def finish(b, m, last):
                pool.wait_ge(h_norm, b * 2 + (m + 1))
                pool.tensor_tensor(x_t[m][:], x_t[m][:], ln_g[:], ALU.mult).then_inc(h_scaled, 1)
                pool.wait_ge(h_scaled, b * 2 + (m + 1))
                pool.tensor_tensor(x_t[m][:], x_t[m][:], ln_b[:], ALU.add).then_inc(h_out, 1)
                pool.wait_ge(h_out, b * 2 + (m + 1))
                pool.dma_start(out[bass.ds(b * BLOCK + m * P, P)], x_t[m][:]).then_inc(out_stored[m], 16)
                pool.wait_ge(out_stored[m], b * 16 + 16)
                if not last:
                    load_x(b + 1, m)

            def body(b, first, last):
                for m in range(2):
                    finish(b, m, last)

            for m in range(2):
                load_x(0, m)
            pool.dma_start(ln_g[:], io["ln_g"].partition_broadcast(P)).then_inc(ln_loaded, 16)
            pool.dma_start(ln_b[:], io["ln_b"].partition_broadcast(P)).then_inc(ln_loaded, 16)
            pool.wait_ge(ln_loaded, 32)
            blocks(pool, body)


def prelude(nc, ident, ident_b, mask):
    with nc.semaphore("made") as made, nc.Block() as block:
        @block.gpsimd
        def _(pool):
            pool.memset(ident[:], 0.0).then_inc(made, 1)
            pool.memset(ident_b[:], 0.0).then_inc(made, 1)
            pool.memset(mask[:], 0.0).then_inc(made, 1)
            pool.wait_ge(made, 3)
            for m in (ident, ident_b):
                pool.affine_select(out=m[:], in_=m[:], compare_op=ALU.not_equal, fill=1.0, base=0,
                                   pattern=[[-1, P]], channel_multiplier=1)
            pool.affine_select(out=mask[:], in_=mask[:], compare_op=ALU.is_ge, fill=-1e30, base=0,
                               pattern=[[-1, P]], channel_multiplier=1)


SCRATCH = {"mixT": (D, S), "silT": (D, S), "qkvT": (3 * D_B, S), "gateT": (3 * D, S), "fcum": (HEADS, S)}


def hybrid_trunk(nc, io, out, stages=3):
    scr = {n: nc.dram_tensor(n, shape, F32, kind="Internal").ap() for n, shape in SCRATCH.items()}
    with ExitStack() as ctx:
        ident = ctx.enter_context(nc.sbuf_tensor("ident", [P, P], F32))
        mask = ctx.enter_context(nc.sbuf_tensor("mask", [P, P], BF16))
        ident_b = ctx.enter_context(nc.sbuf_tensor("ident_b", [P, P], BF16))
        prelude(nc, ident, ident_b, mask)
        with ExitStack() as x_ctx:
            x_hi = x_ctx.enter_context(nc.sbuf_tensor("x_hi", [P, KT, HALF], F32R))
            x_lo, x_raw = low_with_raw(nc, x_ctx, "x_lo", [P, KT, HALF])
            stage_project(nc, io, scr, ident, x_hi, x_lo, x_raw)
            if stages > 1:
                stage_attend(nc, io, scr, ident, ident_b, mask, x_hi, x_lo, x_raw)
        if stages > 2:
            stage_merge(nc, io, scr, out)


def lay_out(inputs):
    a = {k: np.asarray(v)[0] for k, v in inputs.items()}
    cuts = np.cumsum([256, 256, D_B, D_B, D_B, HEADS, D_B, D_C, D_C, 3 * D])
    (za, ga, q, k, v, zf, gb, zc, gc, zg) = np.split(np.arange(cuts[-1]), cuts[:-1])
    cols = np.concatenate([za, ga, gb, gc, q, k, v, zg])
    cf = np.concatenate([zc, zf])
    w, b = a["w_in"], a["b_in"]

    def by_rows(m, width):
        t = m.reshape(m.shape[0] // P, P, m.shape[1] // width, width).transpose(2, 1, 0, 3)
        return np.ascontiguousarray(t).reshape(m.shape[1] // width, P, -1)

    def c(x):
        return np.ascontiguousarray(x)

    edge = np.ones((P, 2, 16), np.float32)
    for n, win in enumerate(WINDOWS):
        t = np.arange(16)
        edge[64 * (n % 2):64 * (n % 2) + 64, n // 2, :] = win / np.minimum(t + 1, win)
    return {
        "xT": c(a["x"].T), "x_tok": c(a["x"]),
        "w_tiles": by_rows(w[:, cols], P), "b_tiles": c(b[cols].reshape(-1, P).T),
        "w_cf": c(w[:, cf].reshape(KT, P, ZCF).transpose(1, 0, 2)), "b_cf": c(b[cf][None]),
        "a_re": c(a["ssm_a_re"].T), "a_im": c(a["ssm_a_im"].T), "log_dt": c(a["ssm_log_dt"][None]),
        "b_re": c(a["ssm_b_re"].transpose(1, 0, 2)), "b_im": c(a["ssm_b_im"].transpose(1, 0, 2)),
        "c_re": c(a["ssm_c_re"].transpose(2, 0, 1)), "c_im": c(a["ssm_c_im"].transpose(2, 0, 1)),
        "d_skip": c(a["ssm_d"].reshape(GROUPS, GC).T),
        "pool_w": c(a["pool_w"]), "pool_scale": c(a["pool_scale"].reshape(2, P).T), "pool_edge": edge,
        "w_glu": c(a["w_glu"].reshape(2, P, D_C).transpose(1, 0, 2)), "b_glu": c(a["b_glu"].reshape(2, P).T),
        "w_up": by_rows(np.concatenate([a["w_up_a"], a["w_up_b"], a["w_up_c"]]), P),
        "w_out": c(a["w_out"].reshape(KT, P, D).transpose(1, 0, 2)),
        "ln_g": c(a["ln_g"][None]), "ln_b": c(a["ln_b"][None]),
    }


def kernel(**inputs):
    import concourse.bacc as bacc
    from concourse.bass_utils import run_bass_kernel_spmd as run

    nc = bacc.Bacc("TRN2", target_bir_lowering=False, num_devices=1)
    arrays = lay_out(inputs)
    io = {n: nc.dram_tensor(f"in_{n}", a.shape, F32, kind="ExternalInput").ap() for n, a in arrays.items()}
    out = nc.dram_tensor("out", (S, D), F32, kind="ExternalOutput").ap()
    hybrid_trunk(nc, io, out)
    r = run(nc, [{f"in_{n}": a for n, a in arrays.items()}], core_ids=[0])
    return r.results[0]["out"].reshape(1, S, D)
```

```python
from contextlib import ExitStack

import numpy as np

import concourse.bass as bass
from concourse import mybir

F32 = mybir.dt.float32
F32R = mybir.dt.float32r
BF16 = mybir.dt.bfloat16
ACT = mybir.ActivationFunctionType
ALU = mybir.AluOpType
AX_X = mybir.AxisListType.X

P = 128
D = 1024
S = 2048
KT = D // P
HALF = S // 2
BANK = 512
NCH = HALF // BANK
WINDOWS = (2, 4, 8, 16)
HEADS = 8
HD = 64
D_B = HEADS * HD
D_C = D // 4
GROUPS, GC = 16, 16
TAU = 8
CHUNKS = HALF // TAU
ALPHA = 2.0 ** 0.25
EPS = 1e-5

T_ZA, T_SIL, T_QKV, T_GATE = 2, 8, 12, 24
T_HALF = T_ZA + T_SIL + T_QKV
ZCF = D_C + HEADS
TWO_PI = 6.283185307179586
PI_A = 6.28125
PI_B = 0.0019350051879882812
PI_C = TWO_PI - PI_A - PI_B
EARLY = 3
ROUND = 1.5 * 2.0 ** 23


def low_with_raw(nc, ctx, name, shape):
    low = ctx.enter_context(nc.sbuf_tensor(name, shape, F32R))
    raw = nc.alloc_sbuf_tensor_at(name + "_raw", shape, F32, offset=nc.sbuf_base - 4 * int(np.prod(shape[1:])))
    return low, raw


def stage_project(nc, io, scr, ident, x_hi, x_lo, x_raw, w_hi, w_lo, w_raw):
    with ExitStack() as ctx:
        def sb(name, shape, dt=F32):
            return ctx.enter_context(nc.sbuf_tensor(name, shape, dt))

        def sem(name):
            return ctx.enter_context(nc.semaphore(name))

        wcf_hi = sb("wcf_hi", [P, KT, ZCF], F32R)
        wcf_lo, wcf_raw = low_with_raw(nc, ctx, "wcf_lo", [P, KT, ZCF])
        bias = sb("bias", [P, T_HALF])
        bcf = sb("bcf", [P, ZCF])
        sig = sb("sig", [P, HALF])
        zout = [sb(f"zout{i}", [P, HALF]) for i in range(2)]
        pool_u = [sb(f"pool_u{i}", [P, 16 + HALF]) for i in range(2)]
        carry = sb("carry", [P, 2, 16])
        pool_w = sb("pool_w", [P, 2, P])
        pool_s = sb("pool_s", [P, 2])
        pool_edge = sb("pool_edge", [P, 2, 16])
        tmp = sb("tmp", [P, 2, 16 + HALF])
        pool_a, pool_b = tmp[:, 0, :], tmp[:, 1, :]
        zs = sb("zs", [P, GROUPS, TAU, GC])
        zs_flat = zs[:].rearrange("p g t h -> p (g t h)")
        zs_y = zs_flat.rearrange("p (t c) -> p t c", t=TAU)
        glu_v = zs_flat.rearrange("p (e t) -> p e t", e=2)
        u_sb = sb("u_sb", [P, GROUPS, CHUNKS])
        yT = u_sb[:].rearrange("p g c -> p (g c)").rearrange("p (j t) -> p j t", j=2)
        xs = sb("xs", [P, GROUPS, CHUNKS + 1])
        xw = sb("xw", [P, GROUPS, CHUNKS + 1])
        m_in = sb("m_in", [P, GROUPS, P])
        m_out = sb("m_out", [P, GROUPS, TAU + 1, GC])
        toep = sb("toep", [P, GROUPS, P])
        kern = xw[0:GC, :, 0:P]
        fcum = m_in[0:HEADS].rearrange("p g c -> p (g c)")
        bx, by, cx, cy, bb, bw = (sb(n, [P, GROUPS, GC]) for n in ("bx", "by", "cx", "cy", "bb", "bw"))
        dT = sb("dT", [GC, GROUPS])
        (are, aim, dt, mag, ang, rnd, red, sn, sh, den, abr, abi, nr, t0, t1, t2, t3, cr, ci) = (
            sb(n, [P, GROUPS]) for n in ("are", "aim", "dt", "mag", "ang", "rnd", "red", "sn", "sh", "den", "abr",
                                         "abi", "nr", "t0", "t1", "t2", "t3", "cr", "ci"))
        pw_r, pw_i, po_r, po_i = (sb(n, [P, GROUPS, TAU + 1]) for n in ("pw_r", "pw_i", "po_r", "po_i"))
        rv_r, rv_i = (sb(n, [P, GROUPS, TAU]) for n in ("rv_r", "rv_i"))
        q_r, q_i, q_s = (sb(n, [P, 7, GROUPS]) for n in ("q_r", "q_i", "q_s"))
        sgn = sb("sgn", [P, 2])
        glu_w = sb("glu_w", [P, 2, D_C])
        glu_b = sb("glu_b", [P, 2])
        zf = sb("zf", [P, 2, TAU, HEADS])
        zf_m = sb("zf_m", [P, 2, TAU, HEADS])
        one = sb("one", [HEADS, 1])

        tile_ps = [ctx.enter_context(nc.psum_tensor(f"tile_ps{i}", [P, HALF], F32)) for i in range(2)]
        aux_ps = [ctx.enter_context(nc.psum_tensor(f"aux_ps{i}", [P, BANK], F32)) for i in range(4)]

        x_loaded = [sem(f"x_loaded{k}") for k in range(KT)]
        w_loaded = [sem(f"w_loaded{i}") for i in range(2)]
        z_stored = [sem(f"z_stored{i}") for i in range(2)]
        (x_split_hi, x_split, w_split_hi, w_split, cf_loaded, cf_split_hi, cf_split, consts, pool_w_zero, pool_w_in,
         tile_done, tile_out, sig_ready, aux_full, aux_free, pool_stored, glu_stored, dve_step, pool_step, dt_ready,
         arg_ready, mag_ready, ang_ready, sin_ready, coefs, in_table, out_table, kern_ready, toep_zero, toep_set,
         pooled, v_ready, scanned, glu_in, glu_sig, glu_out, yT_in, gelu_done, f_arg, f_exp, f_ln,
         f_done, f_stored) = (
            sem(n) for n in (
                "x_split_hi", "x_split", "w_split_hi", "w_split", "cf_loaded", "cf_split_hi", "cf_split", "consts",
                "pool_w_zero", "pool_w_in", "tile_done", "tile_out", "sig_ready", "aux_full", "aux_free",
                "pool_stored", "glu_stored", "dve_step", "pool_step", "dt_ready", "arg_ready", "mag_ready", "ang_ready",
                "sin_ready", "coefs", "in_table", "out_table", "kern_ready", "toep_zero", "toep_set", "pooled",
                "v_ready", "scanned", "glu_in", "glu_sig", "glu_out", "yT_in", "gelu_done", "f_arg",
                "f_exp", "f_ln", "f_done", "f_stored"))

        uses, at = {}, 0
        for hf in range(2):
            first = (("pool", 4), ("u", 4), ("in_table", 4), ("kern", 4), ("v", 4))
            second = (("u", 4), ("v", 4), ("pool", 4), ("forget", 4))
            for name, n in (("cf", TAU), *(second if hf else first), ("y", 4), ("yT", 4), ("glu", 4)):
                uses[name, hf] = at
                at += n

        SMALL = [(bias[:], io["b_tiles"][:, 0:T_HALF]), (bcf[:], io["b_cf"].partition_broadcast(P)),
                 (are[0:64], io["a_re"]), (are[64:P], io["a_re"]), (aim[0:64], io["a_im"]), (aim[64:P], io["a_im"]),
                 (dt[:], io["log_dt"].partition_broadcast(P)),
                 (bx[0:64], io["b_re"]), (bx[64:P], io["b_im"]), (by[0:64], io["b_im"]), (by[64:P], io["b_re"]),
                 (cx[0:64], io["c_re"]), (cx[64:P], io["c_im"]), (cy[0:64], io["c_im"]), (cy[64:P], io["c_re"]),
                 (dT[:], io["d_skip"]), (pool_s[:], io["pool_scale"]), (pool_edge[:], io["pool_edge"]),
                 (glu_w[:], io["w_glu"]), (glu_b[:], io["b_glu"])]
        n_consts = 16 * len(SMALL)

        block = ctx.enter_context(nc.Block())

        @block.sync
        def _(sp):
            def load_w(row, n):
                sp.dma_start(w_raw[n % 2][:], row).then_inc(w_loaded[n % 2], 16)

            def store(dst, hf, u, n):
                sp.wait_ge(tile_out, n + 1)
                sp.dma_start(dst[:, hf * HALF:(hf + 1) * HALF], zout[u][:]).then_inc(z_stored[u], 16)

            w_rows = io["w_tiles"].rearrange("m p (k c) -> (m p) k c", c=P)

            def row(i):
                return w_rows[i * P:(i + 1) * P]

            for hf in range(2):
                n0 = hf * T_HALF
                if hf == 0:
                    load_w(row(0), 0)
                else:
                    sp.wait_ge(tile_done, n0)
                for k in range(KT):
                    sp.dma_start(x_raw[:, k, :],
                                 io["xT"][k * P:(k + 1) * P, hf * HALF:(hf + 1) * HALF]).then_inc(x_loaded[k], 16)
                if hf == 0:
                    load_w(row(1), 1)
                    sp.dma_start(wcf_raw[:], io["w_cf"]).then_inc(cf_loaded, 16)
                for i in range(T_ZA):
                    sp.wait_ge(tile_done, n0 + i + 1)
                    load_w(row(i + 2), n0 + i + 2)
                with sp.Fori(0, T_SIL // 2) as i:
                    for u in range(2):
                        sp.wait_ge(tile_done, i * 2 + (n0 + T_ZA + u + 1))
                        load_w(w_rows[bass.ds(i * (2 * P) + (T_ZA + u + 2) * P, P)], u)
                        store(scr["silT"][bass.ds(i * (2 * P) + u * P, P)], hf, u, i * 2 + (n0 + T_ZA + u))
                with sp.Fori(0, T_QKV // 2 - 1) as i:
                    for u in range(2):
                        sp.wait_ge(tile_done, i * 2 + (n0 + T_ZA + T_SIL + u + 1))
                        load_w(w_rows[bass.ds(i * (2 * P) + (T_ZA + T_SIL + u + 2) * P, P)], u)
                        store(scr["qkvT"][bass.ds(i * (2 * P) + u * P, P)], hf, u, i * 2 + (n0 + T_ZA + T_SIL + u))
                for u in range(2):
                    n = n0 + T_HALF - 2 + u
                    sp.wait_ge(tile_done, n + 1)
                    load_w(row(u + hf * T_HALF), n + 2)
                    store(scr["qkvT"][(T_QKV - 2 + u) * P:(T_QKV - 1 + u) * P], hf, u, n)
            for u in range(2):
                sp.wait_ge(z_stored[u], 16 * (T_SIL + T_QKV))
                sp.wait_ge(w_loaded[u], 16 * (T_HALF + 1))

        @block.scalar
        def _(act):
            def split_w(par, loaded):
                act.wait_ge(w_loaded[par], loaded)
                act.activation(w_hi[par][:], w_raw[par][:], ACT.Copy).then_inc(w_split_hi, 1)

            def split_x(hf, ks):
                for k in ks:
                    act.wait_ge(x_loaded[k], 16 * (hf + 1))
                    act.activation(x_hi[:, k, :], x_raw[:, k, :], ACT.Copy).then_inc(x_split_hi, 1)

            for hf in range(2):
                n0 = hf * T_HALF
                if hf == 0:
                    split_w(0, 16)
                    split_x(0, range(KT))
                    split_w(1, 16)
                    act.wait_ge(cf_loaded, 16)
                    act.activation(wcf_hi[:], wcf_raw[:], ACT.Copy).then_inc(cf_split_hi, 1)
                    for dst, src in SMALL:
                        act.dma_start(dst, src).then_inc(consts, 16)
                for i in range(T_ZA):
                    split_w(i, 8 * n0 + 32)
                if hf == 0:
                    act.wait_ge(consts, n_consts)
                    act.activation(dt[:], dt[:], ACT.Exp).then_inc(dt_ready, 1)
                    act.wait_ge(arg_ready, 1)
                    act.activation(mag[:], mag[:], ACT.Exp).then_inc(mag_ready, 1)
                    act.wait_ge(ang_ready, 1)
                    act.activation(sn[:], red[:], ACT.Sin).then_inc(sin_ready, 1)
                    act.activation(sh[:], red[:], ACT.Sin, scale=0.5).then_inc(sin_ready, 1)
                with act.Fori(0, T_SIL // 2) as i:
                    for u in range(2):
                        act.wait_ge(tile_done, i * 2 + (n0 + T_ZA + u + 1))
                        act.wait_ge(tile_out, i * 2 + (n0 + T_ZA + u))
                        act.activation(sig[:], tile_ps[u][:], ACT.Sigmoid,
                                       bias=bias[:, bass.ds(i * 2 + (T_ZA + u), 1)]).then_inc(sig_ready, 1)
                        split_w(u, i * 16 + (8 * n0 + 48))
                with act.Fori(0, T_QKV // 2 - 2) as i:
                    for u in range(2):
                        split_w(u, i * 16 + (8 * (n0 + T_SIL) + 48))
                if hf == 1:
                    act.wait_ge(f_arg, 1)
                    act.activation(zf[:], zf[:], ACT.Exp, scale=-1.0).then_inc(f_exp, 1)
                    act.wait_ge(f_exp, 1)
                    act.activation(zf[:], zf[:], ACT.Ln, bias=1.0).then_inc(f_ln, 1)
                for u in range(2):
                    split_w(u, 8 * (n0 + T_HALF))
                if hf == 0:
                    split_w(0, 8 * T_HALF + 16)
                for j in range(2):
                    act.wait_ge(yT_in, 2 * (2 * hf + j + 1))
                    act.activation(yT[:, j, :], yT[:, j, :], ACT.Gelu_apprx_tanh).then_inc(gelu_done, 1)
                if hf == 0:
                    split_w(1, 8 * T_HALF + 16)
                    split_x(1, range(KT // 2))
                for e in range(2):
                    act.wait_ge(glu_in, 2 * (2 * hf + e + 1))
                    act.activation(glu_v[:, e, :], glu_v[:, e, :], ACT.Sigmoid).then_inc(glu_sig, 1)
                if hf == 0:
                    split_x(1, range(KT // 2, KT))
                else:
                    split_w(0, 16 * (T_HALF + 1))

        @block.vector
        def _(dve):
            step = [0]

            def link(ins):
                step[0] += 1
                ins.then_inc(dve_step, 1)
                dve.wait_ge(dve_step, step[0])

            def split_w(par, n):
                dve.wait_ge(w_split_hi, n + 1)
                dve.tensor_tensor(w_lo[par][:], w_raw[par][:], w_hi[par][:].bitcast(F32),
                                  ALU.subtract).then_inc(w_split, 1)

            def split_x(hf, ks):
                for k in ks:
                    dve.wait_ge(x_split_hi, hf * KT + k + 1)
                    dve.tensor_tensor(x_lo[:, k, :], x_raw[:, k, :], x_hi[:, k, :].bitcast(F32),
                                      ALU.subtract).then_inc(x_split, 1)

            def bank(name, hf, i):
                n = uses[name, hf] + i
                dve.wait_ge(aux_full, n + 1)
                return aux_ps[n % 4]

            def discretise():
                tt, ts, stt = dve.tensor_tensor, dve.tensor_scalar, dve.scalar_tensor_tensor
                dve.wait_ge(dt_ready, 1)
                tt(mag[:], are[:], dt[:], ALU.mult).then_inc(arg_ready, 1)
                link(tt(ang[:], aim[:], dt[:], ALU.mult))
                link(ts(rnd[:], ang[:], 1.0 / TWO_PI, ROUND, ALU.mult, ALU.add))
                link(ts(rnd[:], rnd[:], -ROUND, None, ALU.add))
                link(stt(red[:], rnd[:], -PI_A, ang[:], ALU.mult, ALU.add))
                link(stt(red[:], rnd[:], -PI_B, red[:], ALU.mult, ALU.add))
                link(stt(red[:], rnd[:], -PI_C, red[:], ALU.mult, ALU.add))
                ts(red[:], red[:], 3.1415925, -3.1415925, ALU.min, ALU.max).then_inc(ang_ready, 1)
                tt(den[:], are[:], are[:], ALU.mult)
                link(tt(t0[:], aim[:], aim[:], ALU.mult))
                link(tt(den[:], den[:], t0[:], ALU.add))
                link(dve.reciprocal(den[:], den[:]))
                dve.wait_ge(mag_ready, 1)
                dve.wait_ge(sin_ready, 2)
                tt(abi[:], mag[:], sn[:], ALU.mult)
                link(stt(t0[:], sh[:], -2.0, sh[:], ALU.mult, ALU.mult))
                link(tt(t0[:], t0[:], mag[:], ALU.mult))
                link(tt(abr[:], t0[:], mag[:], ALU.add))
                link(ts(nr[:], abr[:], -1.0, None, ALU.add))
                tt(t0[:], nr[:], are[:], ALU.mult)
                tt(t1[:], abi[:], aim[:], ALU.mult)
                tt(t2[:], abi[:], are[:], ALU.mult)
                link(tt(t3[:], nr[:], aim[:], ALU.mult))
                tt(t0[:], t0[:], t1[:], ALU.add)
                link(tt(t2[:], t2[:], t3[:], ALU.subtract))
                tt(cr[:], t0[:], den[:], ALU.mult)
                tt(ci[:], t2[:], den[:], ALU.mult).then_inc(coefs, 1)

            def window_sums(hf):
                N = 16 + HALF
                for i in range(2):
                    u = pool_u[i]
                    dve.tensor_copy(carry[:, i, :], u[:, HALF:N])
                    link(dve.tensor_tensor(pool_a[:, 1:N], u[:, 1:N], u[:, 0:N - 1], ALU.add))
                    link(dve.tensor_tensor(pool_b[:, 3:N], pool_a[:, 3:N], pool_a[:, 1:N - 2], ALU.add))
                    if i == 1:
                        link(dve.tensor_tensor(pool_a[:, 7:N], pool_b[:, 7:N], pool_b[:, 3:N - 4], ALU.add))
                        link(dve.tensor_tensor(pool_b[64:P, 15:N], pool_a[64:P, 15:N], pool_a[64:P, 7:N - 8], ALU.add))
                    if hf == 0:
                        dve.tensor_tensor(pool_a[0:64, 16:32], pool_a[0:64, 16:32], pool_edge[0:64, i, :], ALU.mult)
                        link(dve.tensor_tensor(pool_b[64:P, 16:32], pool_b[64:P, 16:32], pool_edge[64:P, i, :],
                                               ALU.mult))
                    dve.scalar_tensor_tensor(u[0:64, 16:N], pool_a[0:64, 16:N], 1.0 / WINDOWS[2 * i],
                                             u[0:64, 16:N], ALU.mult, ALU.subtract)
                    link(dve.scalar_tensor_tensor(u[64:P, 16:N], pool_b[64:P, 16:N], 1.0 / WINDOWS[2 * i + 1],
                                                  u[64:P, 16:N], ALU.mult, ALU.subtract))
                dve.nop().then_inc(pooled, 1)

            def chunk_inputs(hf):
                for i in range(4):
                    ps = bank("u", hf, i)
                    dve.tensor_copy(u_sb[:, 4 * i:4 * i + 4, :].rearrange("p g c -> p (g c)"), ps[:]
                                    ).then_inc(aux_free, 1)

            def state_inputs(hf):
                if hf == 0:
                    dve.wait_ge(toep_set, 16 * TAU)
                    dve.memset(xs[:, :, 0:1], 0.0)
                    link(dve.memset(xw[:, :, 0:1], 0.0))
                for i in range(4):
                    ps = bank("v", hf, i)
                    src = ps[:].rearrange("p (g c) -> p g c", g=4)
                    g4 = slice(4 * i, 4 * i + 4)
                    dve.tensor_copy(xs[:, g4, 1:CHUNKS + 1], src)
                    dve.tensor_copy(xw[0:64, g4, 1:CHUNKS + 1], src[64:P])
                    dve.tensor_copy(xw[64:P, g4, 1:CHUNKS + 1], src[0:64]).then_inc(aux_free, 1)
                dve.wait_ge(aux_free, uses["v", hf] + 4)
                dve.nop().then_inc(v_ready, 1)

            dve.memset(one[:], 1.0)
            for hf in range(2):
                n0 = hf * T_HALF
                if hf == 0:
                    split_w(0, 0)
                    split_x(0, range(KT))
                    split_w(1, 1)
                    dve.wait_ge(cf_split_hi, 1)
                    dve.tensor_tensor(wcf_lo[:], wcf_raw[:], wcf_hi[:].bitcast(F32),
                                      ALU.subtract).then_inc(cf_split, 1)
                    dve.wait_ge(consts, n_consts)
                def pooling_input(i):
                    if hf == 0:
                        dve.memset(pool_u[i][:, 0:16], 0.0)
                    else:
                        dve.wait_ge(pool_stored, 32)
                        dve.tensor_copy(pool_u[i][:, 0:16], carry[:, i, :])
                    dve.wait_ge(tile_done, n0 + i + 1)
                    dve.tensor_scalar(pool_u[i][:, 16:16 + HALF], tile_ps[i][:], bias[:, i:i + 1], None,
                                      ALU.add).then_inc(tile_out, 1)

                pooling_input(0)
                split_w(0, n0 + 2)
                if hf == 0:
                    pooling_input(1)
                    split_w(1, 3)
                for t in range(TAU):
                    ps = bank("cf", hf, t)
                    if hf == 1 and t == 0:
                        dve.wait_ge(glu_stored, 32)
                    dve.tensor_tensor(zs[:, :, t, :], ps[:, 0:D_C].rearrange("p (g h) -> p g h", g=GROUPS),
                                      bcf[:, 0:D_C].rearrange("p (g h) -> p g h", g=GROUPS), ALU.add)
                    dve.tensor_tensor(zf[:, hf, t, :], ps[:, D_C:ZCF], bcf[:, D_C:ZCF],
                                      ALU.add).then_inc(aux_free, 1)
                if hf == 0:
                    discretise()
                else:
                    pooling_input(1)
                    chunk_inputs(1)
                    state_inputs(1)
                    split_w(1, n0 + 3)
                window_sums(hf)

                def gated(i, u, first=False):
                    if not first:
                        dve.wait_ge(z_stored[u], i * 16 + 8 * hf * (T_SIL + T_QKV))
                    dve.wait_ge(sig_ready, i * 2 + (hf * T_SIL + u + 1))
                    dve.scalar_tensor_tensor(zout[u][:], tile_ps[u][:], bias[:, bass.ds(i * 2 + (T_ZA + u), 1)],
                                             sig[:], ALU.add, ALU.mult).then_inc(tile_out, 1)
                    split_w(u, i * 2 + (n0 + T_ZA + u + 2))

                if hf == 0:
                    for u in range(2):
                        gated(0, u, first=True)
                with dve.Fori(1 - hf, T_SIL // 2) as i:
                    for u in range(2):
                        gated(i, u)
                for i in range(4):
                    ps = bank("pool", hf, i)
                    dve.tensor_scalar(pool_u[i // 2][:, 16 + (i % 2) * BANK:16 + (i % 2 + 1) * BANK], ps[:], pool_s[:, i // 2:i // 2 + 1], None,
                                      ALU.mult).then_inc(aux_free, 1)
                if hf == 0:
                    chunk_inputs(0)
                    for i in range(4):
                        ps = bank("in_table", 0, i)
                        dve.tensor_copy(m_in[:, 4 * i:4 * i + 4, :].rearrange("p g c -> p (g c)"),
                                        ps[:]).then_inc(aux_free, 1)
                    for i in range(4):
                        ps = bank("kern", 0, i)
                        dve.tensor_copy(kern[:, 4 * i:4 * i + 4, :], ps[0:GC, :].rearrange("p (g c) -> p g c", g=4)
                                        ).then_inc(aux_free, 1)
                    link(dve.tensor_tensor(bb[0:GC, :, :], ident[0:GC, 0:GC].unsqueeze(1).broadcast_to([GC, GROUPS, GC]),
                                           dT[:].unsqueeze(2).broadcast_to([GC, GROUPS, GC]), ALU.mult))
                    dve.wait_ge(aux_free, uses["kern", 0] + 4)
                    dve.tensor_tensor(kern[:, :, 0:GC], kern[:, :, 0:GC], bb[0:GC, :, :], ALU.add
                                      ).then_inc(kern_ready, 1)
                    state_inputs(0)
                if hf == 1:
                    dve.tensor_scalar(zf_m[:], zf[:], 0.0, None, ALU.min)
                    link(dve.scalar_tensor_tensor(zf[:], zf[:], -1.0, zf[:], ALU.mult, ALU.max))
                    dve.nop().then_inc(f_arg, 1)
                with dve.Fori(0, T_QKV // 2 - 2) as i:
                    for u in range(2):
                        dve.wait_ge(tile_done, i * 2 + (n0 + T_ZA + T_SIL + u + 1))
                        dve.wait_ge(z_stored[u], i * 16 + 8 * (hf * (T_SIL + T_QKV) + T_SIL))
                        dve.tensor_scalar(zout[u][:], tile_ps[u][:], bias[:, bass.ds(i * 2 + (T_ZA + T_SIL + u), 1)],
                                          None, ALU.add).then_inc(tile_out, 1)
                        split_w(u, i * 2 + (n0 + T_ZA + T_SIL + u + 2))

                def tile_from_end(back):
                    u = back % 2
                    n = n0 + T_HALF - back
                    dve.wait_ge(tile_done, n + 1)
                    dve.wait_ge(z_stored[u], 8 * (hf + 1) * (T_SIL + T_QKV) - 16 * ((back + 1) // 2))
                    dve.tensor_scalar(zout[u][:], tile_ps[u][:], bias[:, T_HALF - back:T_HALF - back + 1],
                                      None, ALU.add).then_inc(tile_out, 1)

                def next_split(back):
                    split_w(back % 2, n0 + T_HALF - back + 2)

                def glu_combine():
                    for i in range(4):
                        ps = bank("glu", hf, i)
                        dve.tensor_scalar(glu_v[:, i // 2, (i % 2) * BANK:(i % 2 + 1) * BANK], ps[:],
                                          glu_b[:, i // 2:i // 2 + 1], None, ALU.add).then_inc(glu_in, 1)
                        dve.wait_ge(glu_in, 4 * hf + i + 1)
                        dve.nop().then_inc(aux_free, 1)
                    for e in range(2):
                        dve.wait_ge(glu_sig, 2 * hf + e + 1)
                        dve.tensor_tensor(glu_v[:, e, :], glu_v[:, e, :], yT[:, e, :], ALU.mult).then_inc(glu_out, 1)

                if hf == 0:
                    tile_from_end(4)
                    next_split(4)
                    tile_from_end(3)
                else:
                    dve.wait_ge(f_ln, 1)
                    dve.tensor_tensor(zf_m[:], zf_m[:], zf[:], ALU.subtract).then_inc(f_arg, 1)
                    tile_from_end(4)
                    for i in range(4):
                        ps = bank("forget", 1, i)
                        dst = fcum[:, (i // 2) * HALF:(i // 2 + 1) * HALF].rearrange("p (c t) -> p t c", t=TAU)
                        dve.tensor_copy(dst[:, 4 * (i % 2):4 * (i % 2) + 4, :],
                                        ps[0:HEADS, :].rearrange("p (t c) -> p t c", t=4)).then_inc(aux_free, 1)
                    dve.wait_ge(aux_free, uses["y", 1])
                    dve.tensor_tensor_scan(fcum, one[:].broadcast_to([HEADS, S]), fcum, 0.0, ALU.mult,
                                           ALU.add).then_inc(f_done, 1)
                for i in range(4):
                    ps = bank("y", hf, i)
                    dst = zs_y[:, :, 64 * i:64 * i + 64].rearrange("p t (g h) -> p g t h", g=4)
                    dve.tensor_copy(dst, ps[:].rearrange("p (g t h) -> p g t h", g=4, t=TAU)).then_inc(aux_free, 1)
                if hf == 0:
                    dve.tensor_copy(xs[:, :, 0], xs[:, :, CHUNKS])
                    dve.tensor_copy(xw[:, :, 0], xw[:, :, CHUNKS])
                next_split(4 - (1 - hf))
                tile_from_end(2 + hf)
                for i in range(4):
                    ps = bank("yT", hf, i)
                    dst = yT[:, i // 2, :].rearrange("p (c t) -> p t c", t=TAU)[:, 4 * (i % 2):4 * (i % 2) + 4, :]
                    dve.tensor_copy(dst, ps[:].rearrange("p (t c) -> p t c", t=4)).then_inc(yT_in, 1)
                    dve.wait_ge(yT_in, 4 * hf + i + 1)
                    dve.nop().then_inc(aux_free, 1)
                next_split(2 + hf)
                tile_from_end(1 + hf)
                if hf == 0:
                    next_split(1)
                    split_x(1, range(KT // 2))
                    glu_combine()
                    split_x(1, range(KT // 2, KT))
                else:
                    glu_combine()
                    next_split(2)
                    tile_from_end(1)

        @block.tensor
        def _(pe):
            def open_bank(name, hf, i):
                n = uses[name, hf] + i
                if n >= 4:
                    pe.wait_ge(aux_free, n - 3)
                return aux_ps[n % 4]

            def project(par, n, hf=None):
                pe.wait_ge(w_split, n + 1)
                for k in range(KT):
                    if hf is not None:
                        pe.wait_ge(x_split, hf * KT + k + 1)
                    for j, (w, x) in enumerate(((w_hi, x_hi), (w_lo, x_hi), (w_hi, x_lo))):
                        for c in range(NCH):
                            last = pe.matmul(tile_ps[par][:, c * BANK:(c + 1) * BANK], w[par][:, k, :],
                                             x[:, k, c * BANK:(c + 1) * BANK], start=(k == 0 and j == 0),
                                             stop=(k == KT - 1 and j == 2))
                last.then_inc(tile_done, 1)

            def chunk_inputs(hf):
                pe.wait_ge(aux_free, uses["cf", hf] + TAU)
                for i in range(4):
                    ps = open_bank("u", hf, i)
                    for g in range(4):
                        last = pe.transpose(ps[:, g * P:(g + 1) * P],
                                            zs[:, 4 * i + g].rearrange("p t h -> p (t h)"), ident[:])
                    last.then_inc(aux_full, 1)

            def state_inputs(hf):
                pe.wait_ge(aux_free, uses["u", hf] + 4)
                for i in range(4):
                    ps = open_bank("v", hf, i)
                    for g in range(4):
                        last = pe.matmul(ps[:, g * P:(g + 1) * P], m_in[:, 4 * i + g, :], u_sb[:, 4 * i + g, :],
                                         start=True, stop=True)
                    last.then_inc(aux_full, 1)

            for hf in range(2):
                n0 = hf * T_HALF
                if hf == 1:
                    pe.wait_ge(tile_out, n0 - 1)
                project(0, n0, hf)
                if hf == 0:
                    project(1, 1)
                    pe.wait_ge(cf_split, 1)
                for t in range(TAU):
                    ps = open_bank("cf", hf, t)
                    for k in range(KT):
                        for j, (x, w) in enumerate(((x_hi, wcf_hi), (x_hi, wcf_lo), (x_lo, wcf_hi))):
                            last = pe.matmul(ps[:, 0:ZCF], x[:, k, t:HALF:TAU], w[:, k, :],
                                             start=(k == 0 and j == 0), stop=(k == KT - 1 and j == 2))
                    last.then_inc(aux_full, 1)
                if hf == 1:
                    pe.wait_ge(tile_out, n0)
                    project(1, n0 + 1)
                    chunk_inputs(1)
                    state_inputs(1)
                with pe.Fori(0, T_SIL // 2) as i:
                    for u in range(2):
                        pe.wait_ge(tile_out, i * 2 + (n0 + T_ZA + u - 1))
                        project(u, i * 2 + (n0 + T_ZA + u))
                if hf == 0:
                    pe.wait_ge(pool_w_in, 64)
                pe.wait_ge(pooled, hf + 1)
                for i in range(4):
                    ps = open_bank("pool", hf, i)
                    pe.matmul(ps[:], pool_w[:, i // 2, :], pool_u[i // 2][:, 16 + (i % 2) * BANK:16 + (i % 2 + 1) * BANK],
                              start=True, stop=True).then_inc(aux_full, 1)
                if hf == 0:
                    chunk_inputs(0)
                    pe.wait_ge(in_table, 1)
                    for i in range(4):
                        ps = open_bank("in_table", 0, i)
                        for g in range(4):
                            last = pe.transpose(ps[:, g * P:(g + 1) * P], xs[:, 4 * i + g, 0:P], ident[:])
                        last.then_inc(aux_full, 1)
                    pe.wait_ge(out_table, 1)
                    for i in range(4):
                        ps = open_bank("kern", 0, i)
                        for g in range(4):
                            last = pe.matmul(ps[0:GC, g * P:(g + 1) * P], bb[:, 4 * i + g, :],
                                             m_out[:, 4 * i + g, 0:TAU, :], start=True, stop=True)
                        last.then_inc(aux_full, 1)
                    state_inputs(0)
                with pe.Fori(0, T_QKV // 2 - 2) as i:
                    for u in range(2):
                        pe.wait_ge(tile_out, i * 2 + (n0 + T_ZA + T_SIL + u - 1))
                        project(u, i * 2 + (n0 + T_ZA + T_SIL + u))

                def tile_from_end(back):
                    pe.wait_ge(tile_out, n0 + T_HALF - back - 1)
                    project(back % 2, n0 + T_HALF - back)

                def glu():
                    pe.wait_ge(gelu_done, 2 * (hf + 1))
                    for i in range(4):
                        ps = open_bank("glu", hf, i)
                        e, c = i // 2, i % 2
                        for j in range(2):
                            last = pe.matmul(ps[:], glu_w[:, j, e * P:(e + 1) * P], yT[:, j, c * BANK:(c + 1) * BANK],
                                             start=(j == 0), stop=(j == 1))
                        last.then_inc(aux_full, 1)

                tile_from_end(4)
                if hf == 0:
                    tile_from_end(3)
                if hf == 1:
                    pe.wait_ge(f_arg, 2)
                    for i in range(4):
                        ps = open_bank("forget", 1, i)
                        for t in range(4):
                            last = pe.transpose(ps[0:HEADS, t * P:(t + 1) * P], zf_m[:, i // 2, 4 * (i % 2) + t, :],
                                                ident[:])
                        last.then_inc(aux_full, 1)
                pe.wait_ge(scanned, hf + 1)
                pe.wait_ge(toep_set, 16 * TAU)
                for i in range(4):
                    ps = open_bank("y", hf, i)
                    for g in range(4):
                        pe.matmul(ps[:, g * P:(g + 1) * P], xs[:, 4 * i + g, 0:CHUNKS], m_out[:, 4 * i + g, 1:, :],
                                  start=True, stop=False)
                        last = pe.matmul(ps[:, g * P:(g + 1) * P], u_sb[:, 4 * i + g, :], toep[:, 4 * i + g, :],
                                         start=False, stop=True)
                    last.then_inc(aux_full, 1)
                tile_from_end(2 + hf)
                pe.wait_ge(aux_free, uses["y", hf] + 4)
                for i in range(4):
                    ps = open_bank("yT", hf, i)
                    for t in range(4):
                        last = pe.transpose(ps[:, t * P:(t + 1) * P],
                                            zs_y[:, 4 * (i % 2) + t, (i // 2) * P:(i // 2 + 1) * P], ident[:])
                    last.then_inc(aux_full, 1)
                tile_from_end(1 + hf)
                if hf == 0:
                    glu()
                else:
                    glu()
                    tile_from_end(1)

        @block.gpsimd
        def _(pool):
            step = [0]

            def link(ins):
                step[0] += 1
                ins.then_inc(pool_step, 1)
                pool.wait_ge(pool_step, step[0])

            tt, ts = pool.tensor_tensor, pool.tensor_scalar

            def over_h(a, n):
                return a.unsqueeze(3).broadcast_to([P, a.shape[1], n, GC])

            def over_t(a, n):
                return a.unsqueeze(2).broadcast_to([P, a.shape[1], n, GC])

            def tables():
                pool.memset(pw_r[:, :, 0], 1.0)
                pool.memset(pw_i[:, :, 0], 0.0)
                pool.wait_ge(coefs, 1)
                for k in range(TAU):
                    if k == 0:
                        ts(pw_r[:, :, 1], abr[:], 1.0, None, ALU.mult)
                        link(ts(pw_i[:, :, 1], abi[:], 1.0, None, ALU.mult))
                        continue
                    r, i = pw_r[:, :, k], pw_i[:, :, k]
                    tt(t0[:], r, abr[:], ALU.mult)
                    tt(t1[:], i, abi[:], ALU.mult)
                    tt(t2[:], r, abi[:], ALU.mult)
                    link(tt(t3[:], i, abr[:], ALU.mult))
                    tt(pw_r[:, :, k + 1], t0[:], t1[:], ALU.subtract)
                    link(tt(pw_i[:, :, k + 1], t2[:], t3[:], ALU.add))
                ts(q_r[:, 0, :], pw_r[:, :, TAU], 1.0, None, ALU.mult)
                link(ts(q_i[:, 0, :], pw_i[:, :, TAU], 1.0, None, ALU.mult))
                for j in range(6):
                    r, i = q_r[:, j, :], q_i[:, j, :]
                    tt(t0[:], r, r, ALU.mult)
                    tt(t1[:], i, i, ALU.mult)
                    link(tt(t2[:], r, i, ALU.mult))
                    tt(q_r[:, j + 1, :], t0[:], t1[:], ALU.subtract)
                    link(tt(q_i[:, j + 1, :], t2[:], t2[:], ALU.add))
                ts(q_s[:], q_i[:], sgn[:, 0:1], None, ALU.mult)
                for t in range(TAU):
                    ts(rv_r[:, :, t], pw_r[:, :, TAU - 1 - t], 1.0, None, ALU.mult)
                    ts(rv_i[:, :, t], pw_i[:, :, TAU - 1 - t], sgn[:, 0:1], None, ALU.mult)
                ts(po_r[:], pw_r[:], sgn[:, 1:2], None, ALU.mult)
                ts(po_i[:], pw_i[:], -1.0, None, ALU.mult)
                link(ts(t0[:], ci[:], sgn[:, 0:1], None, ALU.mult))
                r = cr[:].unsqueeze(2).broadcast_to([P, GROUPS, GC])
                i = t0[:].unsqueeze(2).broadcast_to([P, GROUPS, GC])
                h0, h1 = xw[:, :, 0:GC], xw[:, :, GC:2 * GC]
                tt(bb[:], r, bx[:], ALU.mult)
                tt(bw[:], r, by[:], ALU.mult)
                tt(h0, i, by[:], ALU.mult)
                link(tt(h1, i, bx[:], ALU.mult))
                tt(bb[:], bb[:], h0, ALU.add)
                link(tt(bw[:], bw[:], h1, ALU.subtract))
                win = xs[:, :, 0:P].rearrange("p g (t h) -> p g t h", t=TAU)
                part = xw[:, :, 0:P].rearrange("p g (t h) -> p g t h", t=TAU)
                tt(win, over_h(rv_r[:], TAU), over_t(bb[:], TAU), ALU.mult)
                link(tt(part, over_h(rv_i[:], TAU), over_t(bw[:], TAU), ALU.mult))
                tt(win, win, part, ALU.add).then_inc(in_table, 1)
                pool.wait_ge(in_table, 1)
                for g in range(0, GROUPS, 8):
                    g8 = slice(g, g + 8)
                    part = xw[:].rearrange("p g c -> p (g c)")[:, 0:8 * 9 * GC].rearrange(
                        "p (g t h) -> p g t h", g=8, t=TAU + 1)
                    tt(m_out[:, g8], over_h(po_r[:, g8], TAU + 1), over_t(cx[:, g8], TAU + 1), ALU.mult)
                    link(tt(part, over_h(po_i[:, g8], TAU + 1), over_t(cy[:, g8], TAU + 1), ALU.mult))
                    link(tt(m_out[:, g8], m_out[:, g8], part, ALU.add))
                pool.nop().then_inc(out_table, 1)

            def combine(hf, j, dst, src, n):
                cf = wcf_raw[:].rearrange("p k c -> p (k c)")
                other = (cf[:, 0:HALF], cf[:, HALF:2 * HALF]) if hf else (tmp[:, 0, :], tmp[:, 1, :])
                t = [a[:, 0:GROUPS * n] for a in (zs_flat[:, 0:HALF], zs_flat[:, HALF:2 * HALF], *other)]
                t = [a.rearrange("p (g n) -> p g n", g=GROUPS) for a in t]
                r = q_r[:, j, :].unsqueeze(2).broadcast_to([P, GROUPS, n])
                i = q_s[:, j, :].unsqueeze(2).broadcast_to([P, GROUPS, n])
                tt(t[0], xs[:, :, src], r, ALU.mult)
                tt(t[1], xw[:, :, src], i, ALU.mult)
                tt(t[2], xw[:, :, src], r, ALU.mult)
                link(tt(t[3], xs[:, :, src], i, ALU.mult))
                tt(xs[:, :, dst], xs[:, :, dst], t[0], ALU.add)
                link(tt(xw[:, :, dst], xw[:, :, dst], t[2], ALU.add))
                tt(xs[:, :, dst], xs[:, :, dst], t[1], ALU.add)
                link(tt(xw[:, :, dst], xw[:, :, dst], t[3], ALU.subtract))

            def store_mix(row0, now, src, done):
                pool.dma_start(scr["mixT"][row0:row0 + P, now], src).then_inc(done, 16)

            def store_pooled(now, hf):
                pool.wait_ge(aux_free, uses["pool", hf] + 4)
                for i in range(2):
                    store_mix(i * P, now, pool_u[i][:, 16:], pool_stored)

            for rows, c, v in ((slice(0, 64), 0, -1.0), (slice(64, P), 0, 1.0), (slice(0, 64), 1, 1.0),
                               (slice(64, P), 1, -1.0)):
                link(pool.memset(sgn[rows, c:c + 1], v))
            pool.memset(toep[:], 0.0).then_inc(toep_zero, 1)
            pool.memset(pool_w[:], 0.0).then_inc(pool_w_zero, 1)
            pool.wait_ge(pool_w_zero, 1)
            for w in range(4):
                a = 64 * (w % 2)
                pool.dma_start(pool_w[a:a + 64, w // 2, a:a + 64], io["pool_w"][w]).then_inc(pool_w_in, 16)
            for hf in range(2):
                now = slice(hf * HALF, (hf + 1) * HALF)
                if hf == 0:
                    tables()
                    pool.wait_ge(kern_ready, 1)
                    pool.wait_ge(toep_zero, 1)
                    for s in range(TAU):
                        pool.dma_start(toep[GC * s:GC * (s + 1), :, GC * s:P],
                                       kern[:, :, 0:P - GC * s]).then_inc(toep_set, 16)
                if hf == 0:
                    store_pooled(now, 0)
                pool.wait_ge(v_ready, hf + 1)
                combine(hf, 0, slice(1, 2), slice(0, 1), 1)
                for j in range(7):
                    d = 1 << j
                    combine(hf, j, slice(2 * d, CHUNKS + 1, 2 * d), slice(d, CHUNKS + 1 - d, 2 * d), CHUNKS // (2 * d))
                for j in reversed(range(6)):
                    d = 1 << j
                    n = CHUNKS // (2 * d) - 1
                    combine(hf, j, slice(3 * d, 3 * d + 2 * d * (n - 1) + 1, 2 * d),
                            slice(2 * d, 2 * d + 2 * d * (n - 1) + 1, 2 * d), n)
                pool.nop().then_inc(scanned, 1)
                if hf == 1:
                    store_pooled(now, 1)
                    pool.wait_ge(f_done, 1)
                    pool.dma_start(scr["fcum"], fcum).then_inc(f_stored, 16)
                for e in range(2):
                    pool.wait_ge(glu_out, 2 * hf + e + 1)
                    store_mix(D_C + D_B + e * P, now, glu_v[:, e, :], glu_stored)
            pool.wait_ge(pool_stored, 64)
            pool.wait_ge(glu_stored, 64)
            pool.wait_ge(f_stored, 16)


def fill_plan():
    per_piece = 3 * KT
    total = G_TILES * NCH * per_piece
    steps = [(t, j) for t in range(Q_TILES) for j in range(-(-(t + 1) // 4))]
    slots = ["start", *steps, "end", "tail"]
    counts = {s: FILL_BETWEEN for s in steps}
    counts.update({"start": FILL_START, "end": FILL_END, "tail": FILL_TAIL})
    rest = total - sum(counts[s] for s in slots if isinstance(s, str) or s[1])
    rest -= sum(FILL_SHORT)
    for t in range(Q_TILES):
        counts[t, 0] = rest * (t + 1) // Q_TILES - rest * t // Q_TILES
    for t, more in enumerate(FILL_SHORT):
        counts[t, 0] += more
    ends, splits, done = {s: [] for s in slots}, {s: [] for s in slots}, 0
    splits["start"].append(1)
    for n, s in enumerate(slots):
        before, done = done, done + counts[s]
        for piece in range(before // per_piece, done // per_piece):
            ends[s].append(piece)
            if piece % NCH == NCH - 1 and piece // NCH + 2 <= G_TILES:
                later = next(a for a in slots[n + 1:] if isinstance(a, str) or a[1] == 0)
                splits[later].append(piece // NCH + 2)
    assert done == total
    return counts, ends, splits


Q_TILES = S // P
PHASE_HEADS = HEADS // 2
G_TILES = T_GATE // PHASE_HEADS
FILL_SHORT = (9, 6)
FILL_START, FILL_END, FILL_TAIL, FILL_BETWEEN = 30, 16, 22, 3
S_PIECES = sum(-(-(t + 1) // 4) for t in range(Q_TILES))
PT_USES = 2 + S_PIECES


def stage_attend(nc, io, scr, ident, ident_b, mask, x_hi, x_lo, x_raw, gw_hi, gw_lo, gw_raw, early_raw, early_at):
    fill_counts, fill_ends, w_splits = fill_plan()

    with ExitStack() as ctx:
        def sb(name, shape, dt=F32):
            return ctx.enter_context(nc.sbuf_tensor(name, shape, dt))

        def sem(name):
            return ctx.enter_context(nc.semaphore(name))

        g_bias = sb("g_bias", [P, T_GATE])
        g_out = [sb(f"g_out{i}", [P, BANK]) for i in range(NCH)]
        k_hh = sb("k_hh", [P, S], F32R)
        k_ll = sb("k_ll", [P, S], F32R)
        q_st = sb("q_st", [P, S], F32R)
        q_tmp = sb("q_tmp", [P, S], F32R)
        vT = sb("vT", [HD, S])
        v_st = sb("v_st", [P, Q_TILES, 2 * HD], F32R)
        f_row = sb("f_row", [P, S])
        s_sb = [sb(f"s_sb{i}", [P, S]) for i in range(2)]
        mx = [sb(f"mx{i}", [P, 4]) for i in range(2)]
        neg_max = [sb(f"neg_max{i}", [P, 1]) for i in range(2)]
        row_sum = sb("row_sum", [P, Q_TILES])
        row_inv = sb("row_inv", [P, Q_TILES])
        pt_hi = sb("pt_hi", [P, Q_TILES, 2 * P], F32R)
        pt_lo = sb("pt_lo", [P, Q_TILES, 2 * P], F32R)
        o_low = sb("o_low", [HD, 2 * P])
        y_out = [sb(f"y_out{i}", [HD, 2 * P]) for i in range(2)]

        s_ps = [ctx.enter_context(nc.psum_tensor(f"s_ps{i}", [P, BANK], F32)) for i in range(3)]
        t_ps = [ctx.enter_context(nc.psum_tensor(f"t_ps{i}", [P, BANK], F32)) for i in range(2)]
        o_ps = ctx.enter_context(nc.psum_tensor("o_ps", [P, 2, 2 * P], F32))
        g_ps = [ctx.enter_context(nc.psum_tensor(f"g_ps{i}", [P, BANK], F32)) for i in range(NCH)]

        gw_loaded = [sem(f"gw_loaded{i}") for i in range(2)]
        passed = [sem(f"passed{i}") for i in range(3)]
        g_stored = [sem(f"g_stored{i}") for i in range(NCH)]
        y_stored, y_free = sem("y_stored"), sem("y_free")
        x2_loaded = [[sem(f"x2_loaded{c}_{k}") for k in range(0, KT, 2)] for c in range(NCH)]
        x_lo_used, early_loaded = sem("x_lo_used"), sem("early_loaded")
        (x2_hi, x2_split, gb_loaded, gb_half, gw_split_hi, gw_split, g_done, g_ready, kq_loaded, v_loaded, f_loaded, k_hi,
         k_lo, q_hi_tmp, q_hi, q_lo, s_full, s_free, max_ready, p_ready, t_full, t_hi, t_lo, inv_ready, o_full,
         o_low_ready, o_sum, y_ready) = (
            sem(n) for n in (
                "x2_hi", "x2_split", "gb_loaded", "gb_half", "gw_split_hi", "gw_split", "g_done", "g_ready", "kq_loaded",
                "v_loaded", "f_loaded", "k_hi", "k_lo", "q_hi_tmp", "q_hi", "q_lo", "s_full", "s_free", "max_ready",
                "p_ready", "t_full", "t_hi", "t_lo", "inv_ready", "o_full", "o_low_ready", "o_sum", "y_ready"))

        def pieces(t):
            n0 = sum(-(-(a + 1) // 4) for a in range(t))
            keys = (t + 1) * P
            return [(n0 + j, j * BANK, min(BANK, keys - j * BANK)) for j in range(-(-keys // BANK))]

        def pieces_to(t):
            return pieces(t)[-1][0] + 1

        assert nc.sbuf_base <= early_at
        block = ctx.enter_context(nc.Block())

        @block.sync
        def _(sp):
            w_rows = io["w_tiles"].rearrange("m p (k c) -> (m p) k c", c=P)

            def load_w(first_row, par):
                sp.dma_start(gw_raw[par][:], w_rows[bass.ds(first_row, P)]).then_inc(gw_loaded[par], 16)

            def store(row, now, m2, c):
                sp.wait_ge(g_ready, m2 + (NCH + 1))
                sp.dma_start(scr["gateT"][bass.ds(row, P), now + c * BANK:now + (c + 1) * BANK],
                             g_out[c][:]).then_inc(g_stored[c], 16)

            for c in range(NCH):
                sp.sem_inc(g_stored[c], 16)
            sp.dma_start(g_bias[:], io["b_tiles"][:, T_HALF:T_HALF + T_GATE]).then_inc(gb_loaded, 16)
            for u in range(2):
                sp.sem_inc(gw_loaded[u], 16)
            for phase in range(2):
                now = (1 - phase) * HALF
                m0 = phase * T_GATE
                with sp.Fori(0, T_GATE // 2 - 1) as i:
                    for u in range(2):
                        for c in range(NCH):
                            store(i * (2 * P) + u * P, now, i * 4 + (m0 * 2 + 2 * u + c), c)
                        sp.wait_ge(g_done, i * 4 + (m0 * 2 + 2 * u + 2))
                        load_w(i * (2 * P) + (T_HALF + u + 2) * P, u)
                if phase == 1:
                    for i in range(EARLY):
                        sp.dma_start(early_raw[:, i].rearrange("p k c -> p (k c)"), io["w_up"][i]
                                     ).then_inc(early_loaded, 16)
                for u in range(2):
                    for c in range(NCH):
                        if phase == 0 and u == 1:
                            sp.wait_ge(x_lo_used, NCH * T_GATE - NCH + c + 1)
                            for k in range(0, KT, 2):
                                rows = io["xT"][k * P:(k + 2) * P].rearrange("(k p) t -> p k t", p=P)
                                sp.dma_start(x_raw[:, k:k + 2, c * BANK:(c + 1) * BANK],
                                             rows[:, :, c * BANK:(c + 1) * BANK]).then_inc(x2_loaded[c][k // 2], 16)
                        store((T_GATE - 2 + u) * P, now, (m0 + T_GATE - 2 + u) * 2 + c, c)
                    if phase == 0 or u == 0:
                        sp.wait_ge(g_done, (m0 + T_GATE - 1 + u) * 2)
                        load_w((T_HALF + u) * P, u)
            for c in range(NCH):
                sp.wait_ge(g_stored[c], 16 * (2 * T_GATE + 1))
            sp.wait_ge(early_loaded, 16 * EARLY)

        @block.gpsimd
        def _(pool):
            def load_kq(q_row):
                for half in (slice(0, HD), slice(HD, P)):
                    pool.dma_start(k_ll[half].bitcast(F32), scr["qkvT"][bass.ds(q_row + D_B, HD)]).then_inc(kq_loaded, 16)
                    pool.dma_start(q_st[half].bitcast(F32), scr["qkvT"][bass.ds(q_row, HD)]).then_inc(kq_loaded, 16)

            def load_v(q_row):
                pool.dma_start(vT[:], scr["qkvT"][bass.ds(q_row + 2 * D_B, HD)]).then_inc(v_loaded, 16)

            def load_f(h):
                pool.dma_start(f_row[:], scr["fcum"][bass.ds(h, 1)].partition_broadcast(P)).then_inc(f_loaded, 16)

            def store_y(h8, row, p):
                pool.wait_ge(y_ready, h8 + (p + 1))
                pool.dma_start(scr["mixT"][bass.ds(row, HD), p * 2 * P:(p + 1) * 2 * P],
                               y_out[p % 2][:]).then_inc(y_stored, 16)
                pool.wait_ge(y_stored, h8 * 16 + 16 * (p + 1))
                pool.sem_inc(y_free, 1)

            pool.sem_inc(y_free, 2)
            load_kq(0)
            load_v(0)
            load_f(0)
            with pool.Fori(0, HEADS - 1) as h:
                for p in range(6):
                    store_y(h * 8, h * HD + 2 * P, p)
                pool.wait_ge(s_full, h * S_PIECES + S_PIECES)
                load_kq(h * HD + HD)
                store_y(h * 8, h * HD + 2 * P, 6)
                load_v(h * HD + HD)
                pool.wait_ge(s_free, h * S_PIECES + S_PIECES)
                load_f(h + 1)
                store_y(h * 8, h * HD + 2 * P, 7)
            for p in range(8):
                if p == 6:
                    pool.wait_ge(s_full, HEADS * S_PIECES)
                    load_kq(HEADS * HD)
                store_y((HEADS - 1) * 8, (HEADS - 1) * HD + 2 * P, p)

        def phases(eng, before, body):
            for phase in range(2):
                before(phase)
                with eng.Fori(0, PHASE_HEADS) as i:
                    body(lambda k, c: i * k + (c + phase * PHASE_HEADS * k), lambda k, c: i * k + c)

        @block.scalar
        def _(act):
            def split_w(at, j):
                act.wait_ge(gw_loaded[j % 2], at(G_TILES * 8, 16 * (j // 2 + 1)))
                act.activation(gw_hi[j % 2][:], gw_raw[j % 2][:], ACT.Copy).then_inc(gw_split_hi, 1)

            def gates(at, in_phase, slot):
                for j in w_splits[slot]:
                    split_w(at, j)
                for piece in fill_ends[slot]:
                    j, c = divmod(piece, NCH)
                    act.wait_ge(g_done, at(G_TILES * NCH, piece + 1))
                    act.wait_ge(g_stored[c], at(G_TILES * 16, 16 * (j + 1)))
                    act.sem_inc(passed[0])
                    act.activation(g_out[c][:], g_ps[c][:], ACT.Tanh, scale=0.5,
                                   bias=g_bias[:, bass.ds(in_phase(G_TILES, j), 1)]).then_inc(g_ready, 1)

            def low_rows(at, p):
                act.wait_ge(o_full, at(8, p + 1))
                act.activation(o_low[:], o_ps[HD:P, 0, :], ACT.Copy).then_inc(o_low_ready, 1)

            def split_kq(loaded):
                act.wait_ge(kq_loaded, loaded)
                act.activation(k_hh[:], k_ll[:].bitcast(F32), ACT.Copy).then_inc(k_hi, 1)
                act.activation(q_tmp[HD:P], q_st[HD:P].bitcast(F32), ACT.Copy, scale=HD ** -0.5).then_inc(q_hi_tmp, 1)
                act.activation(q_st[0:HD], q_st[0:HD].bitcast(F32), ACT.Copy, scale=HD ** -0.5).then_inc(q_hi, 1)

            def before(phase):
                if phase == 0:
                    act.wait_ge(gb_loaded, 16)
                    act.activation(g_bias[:], g_bias[:], ACT.Copy, scale=0.5).then_inc(gb_half, 1)
                    act.wait_ge(gb_half, 1)
                    act.sem_inc(gw_split_hi, 1)
                    split_kq(64)
                else:
                    act.wait_ge(g_done, NCH * T_GATE)
                    for c in range(NCH):
                        for k in range(KT):
                            cols = slice(c * BANK, (c + 1) * BANK)
                            act.wait_ge(x2_loaded[c][k // 2], 16)
                            act.activation(x_hi[:, k, cols], x_raw[:, k, cols], ACT.Copy).then_inc(x2_hi, 1)

            def body(at, in_phase):
                for b in range(2):
                    act.wait_ge(t_full, at(PT_USES, b + 1))
                    act.activation(v_st[:, 8 * b:8 * b + 8, 0:HD], t_ps[b][:].rearrange("p (t d) -> p t d", t=8),
                                   ACT.Copy).then_inc(t_hi, 1)
                gates(at, in_phase, "start")
                for t in range(Q_TILES):
                    act.wait_ge(max_ready, at(Q_TILES, t + 1))
                    row = s_sb[t % 2][:, 0:(t + 1) * P]
                    act.activation(row, row, ACT.Exp, bias=neg_max[t % 2][:],
                                   accum_out=row_sum[:, t:t + 1]).then_inc(p_ready, 1)
                    gates(at, in_phase, (t, 0))
                    if t % 2 == 0 and t >= 2:
                        low_rows(at, t // 2 - 1)
                    for j, (n, k0, keys) in enumerate(pieces(t)):
                        if j:
                            gates(at, in_phase, (t, j))
                        act.wait_ge(t_full, at(PT_USES, n + 3))
                        act.activation(pt_hi[:, k0 // P:(k0 + keys) // P, (t % 2) * P:(t % 2 + 1) * P],
                                       t_ps[n % 2][:, 0:keys].rearrange("p (k q) -> p k q", q=P),
                                       ACT.Copy).then_inc(t_hi, 1)
                gates(at, in_phase, "end")
                split_kq(at(64, 128))
                low_rows(at, 7)
                gates(at, in_phase, "tail")

            phases(act, before, body)

        @block.vector
        def _(dve):
            def split_w(at, j):
                dve.wait_ge(gw_split_hi, at(G_TILES, j + 1))
                dve.tensor_tensor(gw_lo[j % 2][:], gw_raw[j % 2][:], gw_hi[j % 2][:].bitcast(F32),
                                  ALU.subtract).then_inc(gw_split, 1)

            def logits(at, t):
                for j, (n, k0, keys) in enumerate(pieces(t)):
                    dve.wait_ge(s_full, at(S_PIECES, n + 1))
                    if t >= 2 and j == 0:
                        dve.wait_ge(t_full, at(PT_USES, pieces_to(t - 2) + 2))
                    dve.sem_inc(passed[1])
                    dve.tensor_tensor_reduce(s_sb[t % 2][:, k0:k0 + keys], s_ps[n % 3][:, 0:keys],
                                             f_row[:, k0:k0 + keys], 1.0, -3e38, ALU.subtract, ALU.max,
                                             mx[t % 2][:, j:j + 1]).then_inc(s_free, 1)
                dve.wait_ge(s_free, at(S_PIECES, pieces_to(t)))
                dve.tensor_reduce(neg_max[t % 2][:], mx[t % 2][:, 0:len(pieces(t))], AX_X, ALU.max,
                                  negate=True).then_inc(max_ready, 1)

            def output(at, p):
                dve.wait_ge(o_low_ready, at(8, p + 1))
                dve.wait_ge(y_free, at(8, p + 1))
                y = y_out[p % 2]
                dve.tensor_tensor(y[:], o_ps[0:HD, 0, :], o_low[:], ALU.add).then_inc(o_sum, 1)
                dve.wait_ge(o_sum, at(8, p + 1))
                dve.tensor_tensor(y[:], y[:], o_ps[0:HD, 1, :], ALU.mult).then_inc(y_ready, 1)

            def split_kq(n):
                dve.wait_ge(k_hi, n)
                dve.tensor_tensor(k_ll[:], k_ll[:].bitcast(F32), k_hh[:].bitcast(F32),
                                  ALU.subtract).then_inc(k_lo, 1)
                dve.wait_ge(q_hi_tmp, n)
                dve.scalar_tensor_tensor(q_st[HD:P], q_st[HD:P].bitcast(F32), HD ** -0.5, q_tmp[HD:P].bitcast(F32),
                                         ALU.mult, ALU.subtract).then_inc(q_lo, 1)

            def before(phase):
                if phase == 0:
                    dve.sem_inc(gw_split, 1)
                    split_kq(1)
                else:
                    for c in range(NCH):
                        for k in range(KT):
                            cols = slice(c * BANK, (c + 1) * BANK)
                            dve.wait_ge(x2_hi, c * KT + k + 1)
                            dve.tensor_tensor(x_lo[:, k, cols], x_raw[:, k, cols], x_hi[:, k, cols].bitcast(F32),
                                              ALU.subtract).then_inc(x2_split, 1)

            def body(at, in_phase):
                for b in range(2):
                    dve.wait_ge(t_hi, at(PT_USES, b + 1))
                    v8 = v_st[:, 8 * b:8 * b + 8, :]
                    dve.tensor_tensor(v8[:, :, HD:], t_ps[b][:].rearrange("p (t d) -> p t d", t=8),
                                      v8[:, :, 0:HD].bitcast(F32), ALU.subtract).then_inc(t_lo, 1)
                for j in w_splits["start"]:
                    split_w(at, j)
                dve.wait_ge(f_loaded, at(16, 16))
                logits(at, 0)
                for t in range(Q_TILES):
                    if t + 1 < Q_TILES:
                        logits(at, t + 1)
                    for j in w_splits[t, 0]:
                        split_w(at, j)
                    if t % 2 == 0 and t >= 2:
                        output(at, t // 2 - 1)
                    if t % 2 == 1:
                        dve.wait_ge(p_ready, at(Q_TILES, t + 1))
                        dve.reciprocal(row_inv[:, t - 1:t + 1], row_sum[:, t - 1:t + 1]).then_inc(inv_ready, 1)
                    for n, k0, keys in pieces(t):
                        dve.wait_ge(t_hi, at(PT_USES, n + 3))
                        part = (slice(None), slice(k0 // P, (k0 + keys) // P), slice((t % 2) * P, (t % 2 + 1) * P))
                        dve.tensor_tensor(pt_lo[part], t_ps[n % 2][:, 0:keys].rearrange("p (k q) -> p k q", q=P),
                                          pt_hi[part].bitcast(F32), ALU.subtract).then_inc(t_lo, 1)
                for j in w_splits["end"]:
                    split_w(at, j)
                split_kq(at(1, 2))
                output(at, 7)
                for j in w_splits["tail"]:
                    split_w(at, j)

            phases(dve, before, body)

        @block.tensor
        def _(pe):
            def queries(at, t, part=slice(None)):
                for n, k0, keys in pieces(t)[part]:
                    if n >= 3:
                        pe.wait_ge(s_free, at(S_PIECES, n - 2))
                    ps = s_ps[n % 3][:, 0:keys]
                    last_piece = k0 + keys == (t + 1) * P
                    pe.matmul(ps, q_st[:, t * P:(t + 1) * P], k_hh[:, k0:k0 + keys], start=True, stop=False)
                    last = pe.matmul(ps, q_st[:, t * P:(t + 1) * P], k_ll[:, k0:k0 + keys], start=False,
                                     stop=not last_piece)
                    if last_piece:
                        last = pe.matmul(ps[:, keys - P:keys], ident_b[:], mask[:], start=False, stop=True)
                    last.then_inc(s_full, 1)

            def turn(at, t, fill):
                pe.wait_ge(p_ready, at(Q_TILES, t + 1))
                for j, (n, k0, keys) in enumerate(pieces(t)):
                    if j:
                        fill((t, j))
                    pe.wait_ge(t_lo, at(PT_USES, n + 1))
                    for a in range(keys // P):
                        last = pe.transpose(t_ps[n % 2][:, a * P:(a + 1) * P],
                                            s_sb[t % 2][:, k0 + a * P:k0 + (a + 1) * P], ident[:])
                    last.then_inc(t_full, 1)

            def values(at, p):
                pe.wait_ge(t_lo, at(PT_USES, pieces_to(2 * p + 1) + 2))
                if p:
                    pe.wait_ge(y_ready, at(8, p))
                last_key = 2 * p + 1
                for k in range(last_key + 1):
                    q = slice(P, 2 * P) if k == last_key else slice(0, 2 * P)
                    for j, pt in enumerate((pt_hi, pt_lo)):
                        pe.matmul(o_ps[:, 0, q], v_st[:, k, :], pt[:, k, q], start=(k == 0 and j == 0),
                                  stop=(k == last_key and j == 1))
                pe.wait_ge(inv_ready, at(8, p + 1))
                pe.sem_inc(passed[2])
                for a in range(2):
                    last = pe.transpose(o_ps[0:HD, 1, a * P:(a + 1) * P],
                                        row_inv[:, 2 * p + a:2 * p + a + 1].broadcast_to([P, HD]), ident[:])
                last.then_inc(o_full, 1)

            pe.sem_inc(g_ready, NCH)
            for phase in range(2):
                with pe.Fori(0, PHASE_HEADS) as i:
                    def at(k, c):
                        return i * k + (c + phase * PHASE_HEADS * k)

                    filled = [0]

                    def fill(slot):
                        for _ in range(fill_counts[slot]):
                            piece, r = divmod(filled[0], 3 * KT)
                            j, c = divmod(piece, NCH)
                            k, (w, x) = ((r, (gw_hi, x_lo)) if r < KT else
                                         ((r - KT) // 2, ((gw_hi, x_hi), (gw_lo, x_hi))[(r - KT) % 2]))
                            filled[0] += 1
                            if r == 0:
                                if c == 0:
                                    pe.wait_ge(gw_split, at(G_TILES, j + 1))
                                pe.wait_ge(g_ready, at(G_TILES * NCH, piece + 1))
                            if phase == 1 and j == 0 and r < KT:
                                pe.wait_ge(x2_split, c * KT + k + 1)
                            mm = pe.matmul(g_ps[c][:], w[j % 2][:, k, :], x[:, k, c * BANK:(c + 1) * BANK],
                                           start=(r == 0), stop=(r == 3 * KT - 1))
                            if r == KT - 1:
                                mm.then_inc(x_lo_used, 1)
                            if r == 3 * KT - 1:
                                mm.then_inc(g_done, 1)

                    if phase == 0:
                        fill("start")
                    pe.wait_ge(k_lo, at(1, 1))
                    pe.wait_ge(q_hi, at(1, 1))
                    pe.wait_ge(q_lo, at(1, 1))
                    queries(at, 0)
                    pe.wait_ge(v_loaded, at(16, 16))
                    pe.sem_inc(passed[2])
                    for b in range(2):
                        for t in range(8):
                            k = 8 * b + t
                            last = pe.transpose(t_ps[b][:, t * HD:(t + 1) * HD], vT[:, k * P:(k + 1) * P],
                                                ident[0:HD, 0:HD])
                        last.then_inc(t_full, 1)
                    if phase == 1:
                        fill("start")
                    for t in range(Q_TILES):
                        if t + 1 < Q_TILES:
                            queries(at, t + 1, slice(0, 3))
                        fill((t, 0))
                        if t + 1 < Q_TILES:
                            queries(at, t + 1, slice(3, 4))
                        if t % 2 == 0 and t >= 2:
                            values(at, t // 2 - 1)
                        turn(at, t, fill)
                    fill("end")
                    values(at, 7)
                    fill("tail")


BLOCK = 2 * P
BLOCKS = S // BLOCK
RING = 4
WO_POOL = 5
YG = 4
BRANCH_K = ((0, 2), (2, 6), (6, 8))


def stage_merge(nc, io, scr, out, early_raw, early_at):
    with ExitStack() as ctx:
        def sb(name, shape, dt=F32):
            return ctx.enter_context(nc.sbuf_tensor(name, shape, dt))

        def sem(name):
            return ctx.enter_context(nc.semaphore(name))

        wu_hi, wo_hi = sb("wu_hi", [P, KT, KT, P], F32R), sb("wo_hi", [P, KT, D], F32R)
        wu_lo = [nc.alloc_sbuf_tensor_at(f"wu_lo{i}", [P, KT, P], F32R, offset=early_at + i * KT * P * 4)
                 for i in range(EARLY)]
        wu_raw = [early_raw[:, i] for i in range(EARLY)]
        for i in range(EARLY, KT):
            low, raw = low_with_raw(nc, ctx, f"wu_lo{i}", [P, KT, P])
            wu_lo.append(low)
            wu_raw.append(raw[:])
        wo_lo, wo_raw = low_with_raw(nc, ctx, "wo_lo", [P, KT, D])
        mix = [sb(f"mix{g}", [P, KT // YG, BLOCK]) for g in range(YG)]
        sil = [sb(f"sil{g}", [P, KT // YG, BLOCK]) for g in range(YG)]
        y_hi, y_lo = sb("y_hi", [P, KT, BLOCK], F32R), sb("y_lo", [P, KT, BLOCK], F32R)
        m_hi, m_lo = sb("m_hi", [P, KT, BLOCK], F32R), sb("m_lo", [P, KT, BLOCK], F32R)
        gate = [sb(f"gate{i}", [P, 3, BLOCK]) for i in range(RING)]
        x_t = [sb(f"x_t{m}", [P, D]) for m in range(2)]
        ln_g, ln_b = sb("ln_g", [P, D]), sb("ln_b", [P, D])
        stats = [sb(f"stats{m}", [P, 2, 6]) for m in range(2)]
        mean_var = [sb(f"mean_var{m}", [P, 2]) for m in range(2)]
        fix = [sb(f"fix{m}", [P, 1]) for m in range(2)]
        rstd = [sb(f"rstd{m}", [P, 1]) for m in range(2)]

        u_ps = [ctx.enter_context(nc.psum_tensor(f"u_ps{i}", [P, 4, BLOCK], F32)) for i in range(2)]
        h_ps = [ctx.enter_context(nc.psum_tensor(f"h_ps{m}", [P, D], F32)) for m in range(2)]

        wu_loaded = [sem(f"wu_loaded{i}") for i in range(EARLY, KT)]
        wo_loaded = [sem(f"wo_loaded{i}") for i in range(KT)]
        gate_loaded = [sem(f"gate_loaded{i}") for i in range(RING)]
        mix_loaded = [sem(f"mix_loaded{g}") for g in range(YG)]
        xt_loaded = [sem(f"xt_loaded{m}") for m in range(2)]
        out_stored = [sem(f"out_stored{m}") for m in range(2)]
        (ln_loaded, passed, wu_high, wu_split, wo_high, wo_split, wo_split_v, prod, y_high, y_split, lifted, weighted, part_sum, merged,
         m_high, m_split, h_full, h_sum, h_stats, h_mean, h_var, h_root, h_rstd, h_norm, h_scaled, h_out) = (
            sem(n) for n in (
                "ln_loaded", "passed", "wu_high", "wu_split", "wo_high", "wo_split", "wo_split_v", "prod", "y_high", "y_split", "lifted",
                "weighted", "part_sum", "merged", "m_high", "m_split", "h_full", "h_sum", "h_stats", "h_mean",
                "h_var", "h_root", "h_rstd", "h_norm", "h_scaled", "h_out"))

        def blocks(eng, body):
            body(0, True, False)
            with eng.Fori(1, BLOCKS - 1) as b:
                body(b, False, False)
            body(BLOCKS - 1, False, True)

        def group(t, g):
            return t[:, g * (KT // YG):(g + 1) * (KT // YG)]

        assert nc.sbuf_base <= early_at
        block = ctx.enter_context(nc.Block())

        @block.sync
        def _(sp):
            def load_mix(b):
                for g in range(YG):
                    for dst, src in ((mix[g], scr["mixT"]), (sil[g], scr["silT"])):
                        rows = src[g * (D // YG):(g + 1) * (D // YG)].rearrange("(k p) t -> p k t", p=P)
                        sp.dma_start(dst[:], rows[:, :, bass.ds(b * BLOCK, BLOCK)]).then_inc(mix_loaded[g], 16)

            gates = scr["gateT"].rearrange("(g d p) t -> d p g t", g=3, p=P)

            def load_gate(b, d):
                sp.dma_start(gate[d % RING][:], gates[d][:, :, bass.ds(b * BLOCK, BLOCK)]
                             ).then_inc(gate_loaded[d % RING], 16)

            def load_wu(i):
                sp.dma_start(wu_raw[i].rearrange("p k c -> p (k c)"), io["w_up"][i]
                             ).then_inc(wu_loaded[i - EARLY], 16)

            load_mix(0)
            load_gate(0, 0)
            load_gate(0, 1)
            load_wu(EARLY)
            for d in range(2, RING):
                load_gate(0, d)
            for i in range(EARLY + 1, KT):
                load_wu(i)
            def body(b, first, last):
                if not first and not last:
                    sp.wait_ge(y_split, b * YG + YG)
                    load_mix(b + 1)
                for d in range(KT):
                    sp.wait_ge(m_split, b * KT + (d + 1))
                    if d + RING < KT:
                        load_gate(b, d + RING)
                    elif not last:
                        load_gate(b + 1, d + RING - KT)
                    if first and d < KT // 2:
                        for k in range(2 * d, 2 * d + 2):
                            sp.dma_start(wo_raw[:, k, :], io["w_out"][:, k, :]).then_inc(wo_loaded[k], 16)
                if first:
                    load_mix(1)

            blocks(sp, body)

        @block.scalar
        def _(act):
            def split_wu(i):
                if i >= EARLY:
                    act.wait_ge(wu_loaded[i - EARLY], 16)
                act.activation(wu_hi[:, i], wu_raw[i], ACT.Copy).then_inc(wu_high, 1)

            def split_wo(k):
                act.wait_ge(wo_loaded[k], 16)
                act.activation(wo_hi[:, k], wo_raw[:, k], ACT.Copy).then_inc(wo_high, 1)

            def split_y(b):
                for g in range(YG):
                    act.wait_ge(prod, b * YG + (g + 1))
                    act.activation(group(y_hi, g), mix[g][:], ACT.Copy).then_inc(y_high, 1)

            def root(b, m):
                act.wait_ge(h_var, b * 2 + (m + 1))
                act.activation(rstd[m][:], mean_var[m][:, 1:2], ACT.Sqrt).then_inc(h_root, 1)

            def body(b, first, last):
                for d in range(KT):
                    if first:
                        if d + EARLY < KT:
                            split_wu(d + EARLY)
                    elif d == 3:
                        root(b - 1, 1)
                    act.wait_ge(merged, b * KT + (d + 1))
                    act.activation(m_hi[:, d], gate[d % RING][:, 0], ACT.Copy, scale=0.5).then_inc(m_high, 1)
                    if first and d >= KT // 2:
                        for k in range(2 * d - KT, 2 * d - KT + 2):
                            split_wo(k)
                if not last:
                    split_y(b + 1)
                root(b, 0)

            for i in range(EARLY):
                split_wu(i)
            split_y(0)
            blocks(act, body)
            root(BLOCKS - 1, 1)

        @block.vector
        def _(dve):
            def low(dst, src, hi, done):
                dve.tensor_tensor(dst, src, hi.bitcast(F32), ALU.subtract).then_inc(done, 1)

            def split_y(b):
                def finish(g):
                    dve.wait_ge(y_high, b * YG + (g + 1))
                    low(group(y_lo, g), mix[g][:], group(y_hi, g), y_split)

                for g in range(YG):
                    dve.wait_ge(mix_loaded[g], b * 32 + 32)
                    dve.tensor_tensor(mix[g][:], mix[g][:], sil[g][:], ALU.mult).then_inc(prod, 1)
                    if g:
                        finish(g - 1)
                finish(YG - 1)

            def split_m(b, d):
                dve.wait_ge(m_high, b * KT + (d + 1))
                dve.scalar_tensor_tensor(m_lo[:, d], gate[d % RING][:, 0], 0.5, m_hi[:, d].bitcast(F32), ALU.mult,
                                         ALU.subtract).then_inc(m_split, 1)

            def residual(b, m):
                dve.wait_ge(h_full, b * 2 + (m + 1))
                dve.wait_ge(xt_loaded[m], b * 16 + 16)
                dve.scalar_tensor_tensor(x_t[m][:], x_t[m][:], ALPHA, h_ps[m][:], ALU.mult,
                                         ALU.add).then_inc(h_sum, 1)

            def moments(b, m):
                n = m + 1
                dve.wait_ge(h_sum, b * 2 + n)
                for c in range(2):
                    last = dve.bn_stats(stats[m][:, c, :], x_t[m][:, c * BANK:(c + 1) * BANK])
                last.then_inc(h_stats, 1)
                dve.wait_ge(h_stats, b * 2 + n)
                dve.sem_inc(passed)
                dve.bn_aggr(mean_var[m][:], stats[m][:]).then_inc(h_mean, 1)
                dve.wait_ge(h_mean, b * 2 + n)
                var = mean_var[m][:, 1:2]
                dve.tensor_scalar(var, var, EPS, None, ALU.add).then_inc(h_var, 1)

            def normalise(b, m):
                n = m + 1
                var, r, t = mean_var[m][:, 1:2], rstd[m][:], fix[m][:]
                dve.wait_ge(h_root, b * 2 + n)
                dve.reciprocal(r, r).then_inc(h_rstd, 1)
                dve.wait_ge(h_rstd, b * 8 + (4 * m + 1))
                dve.scalar_tensor_tensor(t, r, var, r, ALU.mult, ALU.mult).then_inc(h_rstd, 1)
                dve.wait_ge(h_rstd, b * 8 + (4 * m + 2))
                dve.tensor_scalar(t, t, -0.5, 1.5, ALU.mult, ALU.add).then_inc(h_rstd, 1)
                dve.wait_ge(h_rstd, b * 8 + (4 * m + 3))
                dve.tensor_tensor(r, r, t, ALU.mult).then_inc(h_rstd, 1)
                dve.wait_ge(h_rstd, b * 8 + (4 * m + 4))
                return dve.tensor_scalar(x_t[m][:], x_t[m][:], mean_var[m][:, 0:1], rstd[m][:], ALU.subtract, ALU.mult)

            def body(b, first, last):
                if not first:
                    residual(b - 1, 1)
                for d in range(KT):
                    dve.wait_ge(lifted, b * KT + (d + 1))
                    dve.wait_ge(gate_loaded[d % RING], b * 32 + 16 * (d // RING + 1))
                    flat = gate[d % RING][:].rearrange("p g t -> p (g t)")
                    dve.scalar_tensor_tensor(flat, flat, 1.0, u_ps[d % 2][:, 0:3].rearrange("p g t -> p (g t)"),
                                             ALU.add, ALU.mult).then_inc(weighted, 1)
                    if not first and d == 3:
                        moments(b - 1, 1)
                    if not first and d == 5:
                        normalise(b - 1, 1).then_inc(h_norm, 1)
                    g = gate[d % RING]
                    dve.wait_ge(weighted, b * KT + (d + 1))
                    dve.tensor_tensor(g[:, 0], g[:, 0], g[:, 1], ALU.add).then_inc(part_sum, 1)
                    if d:
                        split_m(b, d - 1)
                    dve.wait_ge(part_sum, b * KT + (d + 1))
                    dve.tensor_tensor(g[:, 0], g[:, 0], g[:, 2], ALU.add).then_inc(merged, 1)
                split_m(b, KT - 1)
                if first:
                    for k in range(WO_POOL, KT):
                        dve.wait_ge(wo_high, k + 1)
                        low(wo_lo[:, k], wo_raw[:, k], wo_hi[:, k], wo_split_v)
                if not last:
                    split_y(b + 1)
                residual(b, 0)
                moments(b, 0)
                normalise(b, 0).then_inc(h_norm, 1)

            split_y(0)
            blocks(dve, body)
            residual(BLOCKS - 1, 1)
            moments(BLOCKS - 1, 1)
            done = BLOCKS * 8
            normalise(BLOCKS - 1, 1).then_inc(h_rstd, 1)
            dve.wait_ge(ln_loaded, 32)
            dve.wait_ge(h_rstd, done + 1)
            dve.tensor_tensor(x_t[1][:], x_t[1][:], ln_g[:], ALU.mult).then_inc(h_rstd, 1)
            dve.wait_ge(h_rstd, done + 2)
            dve.tensor_tensor(x_t[1][:], x_t[1][:], ln_b[:], ALU.add).then_inc(h_norm, 1)

        @block.tensor
        def _(pe):
            def body(b, first, last):
                for d in range(KT):
                    if first:
                        pe.wait_ge(wu_split, d + 1)
                    if not first or d >= 2:
                        pe.wait_ge(weighted, b * KT + (d - 1))
                    for n, (k0, k1) in enumerate(BRANCH_K):
                        for k in range(k0, k1):
                            if d == 0 and k % (KT // YG) == 0:
                                pe.wait_ge(y_split, b * YG + (k // (KT // YG) + 1))
                            hi, lo = wu_hi[:, d, k, :], wu_lo[d][:, k, :]
                            for j, (w, y) in enumerate(((hi, y_hi), (lo, y_hi), (hi, y_lo))):
                                mm = pe.matmul(u_ps[d % 2][:, n, :], w, y[:, k, :],
                                               start=(k == k0 and j == 0), stop=(k == k1 - 1 and j == 2))
                    mm.then_inc(lifted, 1)
                if not first:
                    pe.wait_ge(h_sum, b * 2)
                for m in range(2):
                    tok = slice(m * P, (m + 1) * P)
                    for k in range(KT):
                        if m == 0:
                            pe.wait_ge(m_split, b * KT + (k + 1))
                            if first:
                                pe.wait_ge(*((wo_split, k + 1) if k < WO_POOL else (wo_split_v, k + 1 - WO_POOL)))
                        for j, (y, w) in enumerate(((m_hi, wo_hi), (m_hi, wo_lo), (m_lo, wo_hi))):
                            for c in range(2):
                                mm = pe.matmul(h_ps[m][:, c * BANK:(c + 1) * BANK], y[:, k, tok],
                                               w[:, k, c * BANK:(c + 1) * BANK], start=(k == 0 and j == 0),
                                               stop=(k == KT - 1 and j == 2))
                    mm.then_inc(h_full, 1)

            blocks(pe, body)

        @block.gpsimd
        def _(pool):
            def load_x(b, m):
                pool.dma_start(x_t[m][:], io["x_tok"][bass.ds(b * BLOCK + m * P, P)]).then_inc(xt_loaded[m], 16)

            def finish(b, m, last):
                pool.wait_ge(h_norm, b * 2 + (m + 1))
                if not (last and m == 1):
                    pool.tensor_tensor(x_t[m][:], x_t[m][:], ln_g[:], ALU.mult).then_inc(h_scaled, 1)
                    pool.wait_ge(h_scaled, b * 2 + (m + 1))
                    pool.tensor_tensor(x_t[m][:], x_t[m][:], ln_b[:], ALU.add).then_inc(h_out, 1)
                    pool.wait_ge(h_out, b * 2 + (m + 1))
                pool.dma_start(out[bass.ds(b * BLOCK + m * P, P)], x_t[m][:]).then_inc(out_stored[m], 16)
                pool.wait_ge(out_stored[m], b * 16 + 16)
                if not last:
                    load_x(b + 1, m)

            def body(b, first, last):
                for m in range(2):
                    finish(b, m, last)

            for i in range(KT):
                pool.wait_ge(wu_high, i + 1)
                pool.tensor_tensor(wu_lo[i][:], wu_raw[i], wu_hi[:, i].bitcast(F32),
                                   ALU.subtract).then_inc(wu_split, 1)
            for k in range(WO_POOL):
                pool.wait_ge(wo_high, k + 1)
                pool.tensor_tensor(wo_lo[:, k], wo_raw[:, k], wo_hi[:, k].bitcast(F32),
                                   ALU.subtract).then_inc(wo_split, 1)
            for m in range(2):
                load_x(0, m)
            pool.dma_start(ln_g[:], io["ln_g"].partition_broadcast(P)).then_inc(ln_loaded, 16)
            pool.dma_start(ln_b[:], io["ln_b"].partition_broadcast(P)).then_inc(ln_loaded, 16)
            pool.wait_ge(ln_loaded, 32)
            blocks(pool, body)


def prelude(nc, ident, ident_b, mask):
    with nc.semaphore("made") as made, nc.Block() as block:
        @block.gpsimd
        def _(pool):
            pool.memset(ident[:], 0.0).then_inc(made, 1)
            pool.memset(ident_b[:], 0.0).then_inc(made, 1)
            pool.memset(mask[:], 0.0).then_inc(made, 1)
            pool.wait_ge(made, 3)
            for m in (ident, ident_b):
                pool.affine_select(out=m[:], in_=m[:], compare_op=ALU.not_equal, fill=1.0, base=0,
                                   pattern=[[-1, P]], channel_multiplier=1)
            pool.affine_select(out=mask[:], in_=mask[:], compare_op=ALU.is_ge, fill=-1e30, base=0,
                               pattern=[[-1, P]], channel_multiplier=1)


SCRATCH = {"mixT": (D, S), "silT": (D, S), "qkvT": (3 * D_B, S), "gateT": (3 * D, S), "fcum": (HEADS, S)}


def hybrid_trunk(nc, io, out, stages=3):
    scr = {n: nc.dram_tensor(n, shape, F32, kind="Internal").ap() for n, shape in SCRATCH.items()}
    with ExitStack() as ctx:
        ident = ctx.enter_context(nc.sbuf_tensor("ident", [P, P], F32))
        mask = ctx.enter_context(nc.sbuf_tensor("mask", [P, P], BF16))
        ident_b = ctx.enter_context(nc.sbuf_tensor("ident_b", [P, P], BF16))
        prelude(nc, ident, ident_b, mask)
        top = nc.sbuf_base + nc.sbuf_bytes_remaining
        early_at = top - EARLY * KT * P * 4
        early_raw = nc.alloc_sbuf_tensor_at("early_raw", [P, EARLY, KT, P], F32, offset=early_at)
        with ExitStack() as x_ctx:
            x_hi = x_ctx.enter_context(nc.sbuf_tensor("x_hi", [P, KT, HALF], F32R))
            x_lo, x_raw = low_with_raw(nc, x_ctx, "x_lo", [P, KT, HALF])
            w_hi = [x_ctx.enter_context(nc.sbuf_tensor(f"w_hi{i}", [P, KT, P], F32R)) for i in range(2)]
            w_lo, w_raw = zip(*(low_with_raw(nc, x_ctx, f"w_lo{i}", [P, KT, P]) for i in range(2)))
            stage_project(nc, io, scr, ident, x_hi, x_lo, x_raw, w_hi, w_lo, w_raw)
            if stages > 1:
                stage_attend(nc, io, scr, ident, ident_b, mask, x_hi, x_lo, x_raw, w_hi, w_lo, w_raw, early_raw, early_at)
        if stages > 2:
            stage_merge(nc, io, scr, out, early_raw, early_at)


def lay_out(inputs):
    a = {k: np.asarray(v)[0] for k, v in inputs.items()}
    cuts = np.cumsum([256, 256, D_B, D_B, D_B, HEADS, D_B, D_C, D_C, 3 * D])
    (za, ga, q, k, v, zf, gb, zc, gc, zg) = np.split(np.arange(cuts[-1]), cuts[:-1])
    cols = np.concatenate([za, ga, gb, gc, q, k, v, zg])
    cf = np.concatenate([zc, zf])
    w, b = a["w_in"], a["b_in"]

    def by_rows(m, width):
        t = m.reshape(m.shape[0] // P, P, m.shape[1] // width, width).transpose(2, 1, 0, 3)
        return np.ascontiguousarray(t).reshape(m.shape[1] // width, P, -1)

    def c(x):
        return np.ascontiguousarray(x)

    edge = np.ones((P, 2, 16), np.float32)
    for n, win in enumerate(WINDOWS):
        t = np.arange(16)
        edge[64 * (n % 2):64 * (n % 2) + 64, n // 2, :] = win / np.minimum(t + 1, win)
    return {
        "xT": c(a["x"].T), "x_tok": c(a["x"]),
        "w_tiles": by_rows(w[:, cols], P), "b_tiles": c(b[cols].reshape(-1, P).T),
        "w_cf": c(w[:, cf].reshape(KT, P, ZCF).transpose(1, 0, 2)), "b_cf": c(b[cf][None]),
        "a_re": c(a["ssm_a_re"].T), "a_im": c(a["ssm_a_im"].T), "log_dt": c(a["ssm_log_dt"][None]),
        "b_re": c(a["ssm_b_re"].transpose(1, 0, 2)), "b_im": c(a["ssm_b_im"].transpose(1, 0, 2)),
        "c_re": c(a["ssm_c_re"].transpose(2, 0, 1)), "c_im": c(a["ssm_c_im"].transpose(2, 0, 1)),
        "d_skip": c(a["ssm_d"].reshape(GROUPS, GC).T),
        "pool_w": c(a["pool_w"]), "pool_scale": c(a["pool_scale"].reshape(2, P).T), "pool_edge": edge,
        "w_glu": c(a["w_glu"].reshape(2, P, D_C).transpose(1, 0, 2)), "b_glu": c(a["b_glu"].reshape(2, P).T),
        "w_up": by_rows(np.concatenate([a["w_up_a"], a["w_up_b"], a["w_up_c"]]), P),
        "w_out": c(a["w_out"].reshape(KT, P, D).transpose(1, 0, 2)),
        "ln_g": c(a["ln_g"][None]), "ln_b": c(a["ln_b"][None]),
    }


def kernel(**inputs):
    import concourse.bacc as bacc
    from concourse.bass_utils import run_bass_kernel_spmd as run

    nc = bacc.Bacc("TRN2", target_bir_lowering=False, num_devices=1)
    arrays = lay_out(inputs)
    io = {n: nc.dram_tensor(f"in_{n}", a.shape, F32, kind="ExternalInput").ap() for n, a in arrays.items()}
    out = nc.dram_tensor("out", (S, D), F32, kind="ExternalOutput").ap()
    hybrid_trunk(nc, io, out)
    r = run(nc, [{f"in_{n}": a for n, a in arrays.items()}], core_ids=[0])
    return r.results[0]["out"].reshape(1, S, D)
```
